# Optimizing a Trainium2 kernel written in Bass

```python
import math
import jax, jax.numpy as jnp
from jax import lax
import numpy as np

D_MODEL = 1024
BATCH = 1
SEQ = 1024
DEPTH = 1

N_META = 16
ATTN_WIDTH = D_MODEL // 2
SSM_WIDTH = D_MODEL - ATTN_WIDTH
N_ATTN_HEADS = 4
QK_DIM = ATTN_WIDTH // N_ATTN_HEADS // 2
V_DIM = 2 * QK_DIM
ROT_DIM = QK_DIM // 4
ROPE_THETA = 500000.0
SSM_GROUP = 16
N_SSM_GROUPS = SSM_WIDTH // SSM_GROUP
SSM_STATE = 64
D_FF = -(-8 * D_MODEL // (3 * 256)) * 256
Q_BLOCK = 128
EPS = 1e-6
QK_COLS = N_ATTN_HEADS * QK_DIM
V_COLS = N_ATTN_HEADS * V_DIM
IN_COLS = 4 * QK_COLS + V_COLS + SSM_WIDTH


def rms_norm(x, g):
    x32 = x.astype(jnp.float32)
    y = x32 * lax.rsqrt(jnp.mean(x32 * x32, axis=-1, keepdims=True) + EPS)
    return (y * g.astype(jnp.float32)).astype(x.dtype)

def lambda_init(layer_idx):
    return 0.8 - 0.6 * math.exp(-0.3 * layer_idx)

def rope_tables(length):
    pos = jnp.arange(length, dtype=jnp.float32)
    inv_freq = ROPE_THETA ** (-jnp.arange(0, ROT_DIM, 2, dtype=jnp.float32) / ROT_DIM)
    ang = pos[:, None] * inv_freq[None, :]
    ang = jnp.concatenate([ang, ang], axis=-1)
    return jnp.cos(ang), jnp.sin(ang)

def partial_rope(t, cos, sin):
    t_rot, t_pass = t[..., :ROT_DIM], t[..., ROT_DIM:]
    half = ROT_DIM // 2
    rot_half = jnp.concatenate([-t_rot[..., half:], t_rot[..., :half]], axis=-1)
    t_rot = (t_rot * cos + rot_half * sin).astype(t.dtype)
    return jnp.concatenate([t_rot, t_pass], axis=-1)

def diff_attention(q1, q2, k1, k2, v, lam):
    b, h, lp, d = q1.shape
    nb = lp // Q_BLOCK
    scale = 1.0 / math.sqrt(d)
    k_pos = jnp.arange(lp)
    v32 = v.astype(jnp.float32)

    def to_blocks(t):
        return t.reshape(b, h, nb, Q_BLOCK, t.shape[-1]).transpose(2, 0, 1, 3, 4)

    def block(args):
        q1b, q2b, start = args
        q_pos = start + jnp.arange(Q_BLOCK)
        causal = k_pos[None, :] <= q_pos[:, None]

        def probs(qb, k):
            s = jnp.einsum('bhqd,bhkd->bhqk', qb, k, preferred_element_type=jnp.float32) * scale
            return jax.nn.softmax(jnp.where(causal, s, -jnp.inf), axis=-1)

        attn = probs(q1b, k1) - lam * probs(q2b, k2)
        return jnp.einsum('bhqk,bhkd->bhqd', attn, v32)

    starts = jnp.arange(nb, dtype=jnp.int32) * Q_BLOCK
    out = lax.map(block, (to_blocks(q1), to_blocks(q2), starts))
    return out.transpose(1, 2, 0, 3, 4).reshape(b, h, lp, v.shape[-1])

def s5_ssm(u, a_re, a_im, log_dt, b_re, b_im, c_re, c_im, d_skip):
    u = u.astype(jnp.float32)
    dt = jnp.exp(log_dt.astype(jnp.float32))[:, None]
    a_re = a_re.astype(jnp.float32)
    a_im = a_im.astype(jnp.float32)
    mag = jnp.exp(a_re * dt)
    ang = a_im * dt
    ab_re, ab_im = mag * jnp.cos(ang), mag * jnp.sin(ang)
    den = a_re * a_re + a_im * a_im
    nr, ni = ab_re - 1.0, ab_im
    f_re = (nr * a_re + ni * a_im) / den
    f_im = (ni * a_re - nr * a_im) / den
    b_re = b_re.astype(jnp.float32)
    b_im = b_im.astype(jnp.float32)
    bb_re = f_re[..., None] * b_re - f_im[..., None] * b_im
    bb_im = f_re[..., None] * b_im + f_im[..., None] * b_re
    bu_re = jnp.einsum('blgh,gph->blgp', u, bb_re)
    bu_im = jnp.einsum('blgh,gph->blgp', u, bb_im)
    ar = jnp.broadcast_to(ab_re, bu_re.shape)
    ai = jnp.broadcast_to(ab_im, bu_re.shape)

    def combine(e1, e2):
        ar1, ai1, br1, bi1 = e1
        ar2, ai2, br2, bi2 = e2
        return (ar2 * ar1 - ai2 * ai1,
                ar2 * ai1 + ai2 * ar1,
                ar2 * br1 - ai2 * bi1 + br2,
                ar2 * bi1 + ai2 * br1 + bi2)

    _, _, x_re, x_im = lax.associative_scan(combine, (ar, ai, bu_re, bu_im), axis=1)
    y = (jnp.einsum('blgp,ghp->blgh', x_re, c_re.astype(jnp.float32))
         - jnp.einsum('blgp,ghp->blgh', x_im, c_im.astype(jnp.float32)))
    y = y + d_skip.astype(jnp.float32).reshape(N_SSM_GROUPS, SSM_GROUP) * u
    bsz, length = u.shape[0], u.shape[1]
    return y.reshape(bsz, length, N_SSM_GROUPS * SSM_GROUP)

def first_inputs(seed: int = 0) -> dict:
    key = jax.random.key(seed)
    ks = jax.random.split(key, 32)
    f32 = jnp.float32

    def nrm(k, shape, scale):
        return jax.random.normal(k, shape, f32) * scale

    def gain(k, shape):
        return 1.0 + 0.02 * jax.random.normal(k, shape, f32)

    n_idx = jnp.arange(SSM_STATE, dtype=f32)
    a_re = -0.5 + 0.01 * jax.random.normal(ks[8], (DEPTH, N_SSM_GROUPS, SSM_STATE), f32)
    a_im = math.pi * n_idx[None, None, :] + 0.01 * jax.random.normal(ks[9], (DEPTH, N_SSM_GROUPS, SSM_STATE), f32)
    log_dt = jax.random.uniform(ks[10], (DEPTH, N_SSM_GROUPS), f32, math.log(1e-3), math.log(1e-1))
    return {
        "x": nrm(ks[0], (BATCH, SEQ, D_MODEL), 1.0),
        "meta": nrm(ks[1], (N_META, D_MODEL), 1.0),
        "pre_mix_g": gain(ks[2], (DEPTH, D_MODEL)),
        "w_in": nrm(ks[3], (DEPTH, D_MODEL, IN_COLS), D_MODEL ** -0.5),
        "lambda_q1": nrm(ks[4], (DEPTH, QK_DIM), 0.1),
        "lambda_k1": nrm(ks[5], (DEPTH, QK_DIM), 0.1),
        "lambda_q2": nrm(ks[6], (DEPTH, QK_DIM), 0.1),
        "lambda_k2": nrm(ks[7], (DEPTH, QK_DIM), 0.1),
        "subln_g": gain(ks[11], (DEPTH, V_DIM)),
        "a_re": a_re,
        "a_im": a_im,
        "log_dt": log_dt,
        "b_re": nrm(ks[12], (DEPTH, N_SSM_GROUPS, SSM_STATE, SSM_GROUP), (2.0 * SSM_GROUP) ** -0.5),
        "b_im": nrm(ks[13], (DEPTH, N_SSM_GROUPS, SSM_STATE, SSM_GROUP), (2.0 * SSM_GROUP) ** -0.5),
        "c_re": nrm(ks[14], (DEPTH, N_SSM_GROUPS, SSM_GROUP, SSM_STATE), (2.0 * SSM_STATE) ** -0.5),
        "c_im": nrm(ks[15], (DEPTH, N_SSM_GROUPS, SSM_GROUP, SSM_STATE), (2.0 * SSM_STATE) ** -0.5),
        "d_skip": nrm(ks[16], (DEPTH, SSM_WIDTH), 1.0),
        "w_glu": nrm(ks[17], (DEPTH, SSM_WIDTH, SSM_WIDTH), SSM_WIDTH ** -0.5),
        "b_glu": nrm(ks[18], (DEPTH, SSM_WIDTH), 0.02),
        "ssm_out_g": gain(ks[19], (DEPTH, SSM_WIDTH)),
        "w_out": nrm(ks[20], (DEPTH, D_MODEL, D_MODEL), D_MODEL ** -0.5),
        "post_mix_g": gain(ks[21], (DEPTH, D_MODEL)),
        "pre_ffn_g": gain(ks[22], (DEPTH, D_MODEL)),
        "w_gate": nrm(ks[23], (DEPTH, D_MODEL, D_FF), D_MODEL ** -0.5),
        "w_up": nrm(ks[24], (DEPTH, D_MODEL, D_FF), D_MODEL ** -0.5),
        "w_down": nrm(ks[25], (DEPTH, D_FF, D_MODEL), D_FF ** -0.5),
        "post_ffn_g": gain(ks[26], (DEPTH, D_MODEL)),
    }

def first_block(x, meta, pre_mix_g, w_in, lambda_q1, lambda_k1, lambda_q2, lambda_k2, subln_g,
              a_re, a_im, log_dt, b_re, b_im, c_re, c_im, d_skip, w_glu, b_glu, ssm_out_g,
              w_out, post_mix_g, pre_ffn_g, w_gate, w_up, w_down, post_ffn_g):
    bsz = x.shape[0]
    meta_b = jnp.broadcast_to(meta.astype(x.dtype)[None], (bsz, N_META, x.shape[-1]))
    h_res = jnp.concatenate([meta_b, x], axis=1)
    length = h_res.shape[1]
    l_pad = -(-length // Q_BLOCK) * Q_BLOCK
    cos, sin = rope_tables(length)

    def heads(t, dim):
        t = t.reshape(bsz, length, N_ATTN_HEADS, dim).transpose(0, 2, 1, 3)
        return t

    def pad(t):
        return jnp.pad(t, ((0, 0), (0, 0), (0, l_pad - length), (0, 0)))

    for l in range(DEPTH):
        lam_init = lambda_init(l)
        h = rms_norm(h_res, pre_mix_g[l])
        proj = jnp.einsum('bld,dc->blc', h, w_in[l])
        q1, q2, k1, k2, v, u = jnp.split(
            proj, [QK_COLS, 2 * QK_COLS, 3 * QK_COLS, 4 * QK_COLS, 4 * QK_COLS + V_COLS], axis=-1)

        q1 = pad(partial_rope(heads(q1, QK_DIM), cos, sin))
        q2 = pad(partial_rope(heads(q2, QK_DIM), cos, sin))
        k1 = pad(partial_rope(heads(k1, QK_DIM), cos, sin))
        k2 = pad(partial_rope(heads(k2, QK_DIM), cos, sin))
        vh = pad(heads(v, V_DIM))
        lam = (jnp.exp(jnp.sum(lambda_q1[l].astype(jnp.float32) * lambda_k1[l].astype(jnp.float32)))
               - jnp.exp(jnp.sum(lambda_q2[l].astype(jnp.float32) * lambda_k2[l].astype(jnp.float32)))
               + lam_init)
        o = diff_attention(q1, q2, k1, k2, vh, lam)[:, :, :length]
        o = rms_norm(o, subln_g[l]) * (1.0 - lam_init)
        o = o.transpose(0, 2, 1, 3).reshape(bsz, length, V_COLS).astype(h.dtype)

        y = s5_ssm(u.reshape(bsz, length, N_SSM_GROUPS, SSM_GROUP), a_re[l], a_im[l], log_dt[l],
                   b_re[l], b_im[l], c_re[l], c_im[l], d_skip[l])
        y = jax.nn.gelu(y, approximate=False)
        y = y * jax.nn.sigmoid(jnp.einsum('blc,cd->bld', y, w_glu[l].astype(jnp.float32))
                               + b_glu[l].astype(jnp.float32))
        y = rms_norm(y, ssm_out_g[l]).astype(h.dtype)

        mix = jnp.einsum('blc,cd->bld', jnp.concatenate([o, y], axis=-1), w_out[l])
        h_res = h_res + rms_norm(mix, post_mix_g[l])

        h = rms_norm(h_res, pre_ffn_g[l])
        f = jax.nn.silu(jnp.einsum('bld,df->blf', h, w_gate[l])) * jnp.einsum('bld,df->blf', h, w_up[l])
        f = jnp.einsum('blf,fd->bld', f, w_down[l])
        h_res = h_res + rms_norm(f, post_ffn_g[l])

    return h_res[:, N_META:]


_first_inputs = first_inputs


def first_inputs(seed=0):
    import zlib

    import numpy as np

    out = dict(_first_inputs(seed))
    spreads = {}
    factors = {}
    for name, (base, spread) in spreads.items():
        noise = np.random.default_rng([zlib.crc32(name.encode()), seed]).standard_normal(out[name].shape)
        drawn = base * np.exp(spread * noise) if base else spread * noise
        out[name] = __import__('jax').numpy.asarray(drawn.astype(out[name].dtype))
    for name, factor in factors.items():
        out[name] = (out[name] * factor).astype(out[name].dtype)
    return out


_narrow_inputs = first_inputs


def first_inputs(seed=0):
    out = dict(_narrow_inputs(seed))
    wider = {'lambda_k1': 3.91,
     'lambda_q2': 4.15,
     'subln_g': 5.71,
     'a_re': 12.0,
     'b_glu': 12.0,
     'ssm_out_g': 5.52,
     'post_mix_g': 3.74,
     'pre_ffn_g': 3.85,
     'post_ffn_g': 5.46}
    for name, times in wider.items():
        mean = out[name].mean()
        out[name] = (mean + times * (out[name] - mean)).astype(out[name].dtype)
    return out


MIX_WIDTH = D_MODEL
HEAD_DIM = 64
A_WIDTH = MIX_WIDTH // 2
B_WIDTH = MIX_WIDTH - A_WIDTH
A_GROUPS = A_WIDTH // HEAD_DIM
A_GROUP_DIM = A_WIDTH // A_GROUPS
B_HEADS = B_WIDTH // HEAD_DIM
CHUNK = 128
D_FF_2 = ((8 * D_MODEL // 3 + 255) // 256) * 256
COL_A_U = 0
COL_A_V = COL_A_U + A_WIDTH
COL_B_Q = COL_A_V + A_WIDTH
COL_B_K = COL_B_Q + B_WIDTH
COL_B_V = COL_B_K + B_WIDTH
COL_B_F = COL_B_V + B_WIDTH
IN_COLS_2 = COL_B_F + B_HEADS
RMS_EPS = 1e-6
LN_EPS = 1e-5


def _rmsnorm(x, g):
    x32 = x.astype(jnp.float32)
    y = x32 * lax.rsqrt(jnp.mean(x32 * x32, axis=-1, keepdims=True) + RMS_EPS)
    return (y * g.astype(jnp.float32)).astype(x.dtype)

def _layernorm(x, g, b):
    x32 = x.astype(jnp.float32)
    mu = jnp.mean(x32, axis=-1, keepdims=True)
    var = jnp.mean(jnp.square(x32 - mu), axis=-1, keepdims=True)
    y = (x32 - mu) * lax.rsqrt(var + LN_EPS)
    return (y * g.astype(jnp.float32) + b.astype(jnp.float32)).astype(x.dtype)

def _spatial_gating(u, v, ln_g, ln_b, w_s, b_s):
    B, S, _ = v.shape
    nc = S // CHUNK
    v = _layernorm(v, ln_g, ln_b)
    v = v.reshape(B, nc, CHUNK, A_GROUPS, A_GROUP_DIM)
    tril = jnp.tril(jnp.ones((CHUNK, CHUNK), dtype=w_s.dtype))
    w_masked = w_s * tril[None]
    mixed = jnp.einsum('gts,bcsgd->bctgd', w_masked, v) + b_s.T[None, None, :, :, None]
    out = u.reshape(B, nc, CHUNK, A_GROUPS, A_GROUP_DIM) * mixed
    return out.reshape(B, S, A_WIDTH)

def _forgetting_attention(q, k, v, f_logit, b_f):
    B, S, _ = q.shape
    def heads(t):
        return t.reshape(B, S, B_HEADS, HEAD_DIM).transpose(0, 2, 1, 3)
    q, k, v = heads(q), heads(k), heads(v)
    log_f = jax.nn.log_sigmoid(f_logit.astype(jnp.float32) + b_f.astype(jnp.float32))
    c = jnp.cumsum(log_f, axis=1).transpose(0, 2, 1)
    scale = HEAD_DIM ** -0.5
    pos = jnp.arange(S)
    outs = []
    for i in range(S // Q_BLOCK):
        q0, q1 = i * Q_BLOCK, (i + 1) * Q_BLOCK
        q_blk = q[:, :, q0:q1]
        k_blk = k[:, :, :q1]
        v_blk = v[:, :, :q1]
        logits = jnp.einsum('bhqd,bhkd->bhqk', q_blk, k_blk).astype(jnp.float32) * scale
        logits = logits + c[:, :, q0:q1, None] - c[:, :, None, :q1]
        mask = pos[q0:q1, None] >= pos[None, :q1]
        logits = jnp.where(mask[None, None], logits, -jnp.inf)
        p = jax.nn.softmax(logits, axis=-1).astype(v.dtype)
        outs.append(jnp.einsum('bhqk,bhkd->bhqd', p, v_blk))
    o = jnp.concatenate(outs, axis=2)
    return o.transpose(0, 2, 1, 3).reshape(B, S, B_WIDTH)

def second_inputs(seed: int = 0) -> dict:
    key = jax.random.key(seed)
    ks = jax.random.split(key, 20)
    f32 = jnp.float32
    L = DEPTH
    def nrm(k, shape, scale):
        return jax.random.normal(k, shape, f32) * scale
    return {
        "x": jax.random.normal(ks[0], (BATCH, SEQ, D_MODEL), f32),
        "pre_mix_gain": 1.0 + nrm(ks[1], (L, D_MODEL), 0.02),
        "w_in": nrm(ks[2], (L, D_MODEL, IN_COLS_2), D_MODEL ** -0.5),
        "ln_v_gain": 1.0 + nrm(ks[3], (L, A_WIDTH), 0.02),
        "ln_v_bias": nrm(ks[4], (L, A_WIDTH), 0.02),
        "w_spatial": nrm(ks[5], (L, A_GROUPS, CHUNK, CHUNK), 0.5 * CHUNK ** -0.5),
        "b_spatial": 1.0 + nrm(ks[6], (L, A_GROUPS, CHUNK), 0.1),
        "b_forget": 2.0 + nrm(ks[7], (L, B_HEADS), 0.5),
        "out_norm_a_gain": 1.0 + nrm(ks[8], (L, A_WIDTH), 0.02),
        "out_norm_b_gain": 1.0 + nrm(ks[9], (L, B_WIDTH), 0.02),
        "w_out": nrm(ks[10], (L, MIX_WIDTH, D_MODEL), MIX_WIDTH ** -0.5),
        "post_mix_gain": 1.0 + nrm(ks[11], (L, D_MODEL), 0.02),
        "pre_ffn_gain": 1.0 + nrm(ks[12], (L, D_MODEL), 0.02),
        "w_ffn_in": nrm(ks[13], (L, D_MODEL, 2 * D_FF_2), D_MODEL ** -0.5),
        "w_ffn_out": nrm(ks[14], (L, D_FF_2, D_MODEL), D_FF_2 ** -0.5),
        "post_ffn_gain": 1.0 + nrm(ks[15], (L, D_MODEL), 0.02),
    }

def second_block(x, pre_mix_gain, w_in, ln_v_gain, ln_v_bias, w_spatial, b_spatial,
              b_forget, out_norm_a_gain, out_norm_b_gain, w_out, post_mix_gain,
              pre_ffn_gain, w_ffn_in, w_ffn_out, post_ffn_gain):
    h = x
    for l in range(DEPTH):
        n = _rmsnorm(h, pre_mix_gain[l])
        proj = jnp.einsum('bsd,dc->bsc', n, w_in[l])
        a_u = jax.nn.gelu(proj[..., COL_A_U:COL_A_V], approximate=False)
        a_v = jax.nn.gelu(proj[..., COL_A_V:COL_B_Q], approximate=False)
        a_out = _spatial_gating(a_u, a_v, ln_v_gain[l], ln_v_bias[l],
                                w_spatial[l], b_spatial[l])
        b_out = _forgetting_attention(proj[..., COL_B_Q:COL_B_K],
                                      proj[..., COL_B_K:COL_B_V],
                                      proj[..., COL_B_V:COL_B_F],
                                      proj[..., COL_B_F:IN_COLS_2],
                                      b_forget[l])
        merged = jnp.concatenate([_rmsnorm(a_out, out_norm_a_gain[l]),
                                  _rmsnorm(b_out, out_norm_b_gain[l])], axis=-1)
        mix = jnp.einsum('bsc,cd->bsd', merged, w_out[l])
        h = h + _rmsnorm(mix, post_mix_gain[l])
        n2 = _rmsnorm(h, pre_ffn_gain[l])
        gu = jnp.einsum('bsd,df->bsf', n2, w_ffn_in[l])
        ff = jax.nn.silu(gu[..., :D_FF_2]) * gu[..., D_FF_2:]
        ff = jnp.einsum('bsf,fd->bsd', ff, w_ffn_out[l])
        h = h + _rmsnorm(ff, post_ffn_gain[l])
    return h


_first_inputs_2 = second_inputs


def second_inputs(seed=0):
    import zlib

    import numpy as np

    out = dict(_first_inputs_2(seed))
    spreads = {}
    factors = {'ln_v_gain': 8.0,
     'ln_v_bias': 8.0,
     'out_norm_a_gain': 5.117,
     'out_norm_b_gain': 4.957,
     'post_mix_gain': 3.435,
     'pre_ffn_gain': 3.481,
     'post_ffn_gain': 4.955}
    for name, (base, spread) in spreads.items():
        noise = np.random.default_rng([zlib.crc32(name.encode()), seed]).standard_normal(out[name].shape)
        drawn = base * np.exp(spread * noise) if base else spread * noise
        out[name] = __import__('jax').numpy.asarray(drawn.astype(out[name].dtype))
    for name, factor in factors.items():
        out[name] = (out[name] * factor).astype(out[name].dtype)
    return out


_narrow_inputs_2 = second_inputs


def second_inputs(seed=0):

    out = dict(_narrow_inputs_2(seed))
    wider = {'ln_v_gain': 4.2,
     'ln_v_bias': 4.13,
     'out_norm_a_gain': 3.75,
     'out_norm_b_gain': 3.74,
     'post_ffn_gain': 3.97}
    for name, times in wider.items():
        mean = out[name].mean()
        out[name] = (mean + times * (out[name] - mean)).astype(out[name].dtype)
    return out


def setup_inputs(seed=0):
    out = dict(first_inputs(seed))
    for name, value in second_inputs(seed + 1).items():
        if name != "x":
            out[name + "_2"] = value
    return out


def reference(
    x, meta, pre_mix_g, w_in, lambda_q1, lambda_k1, lambda_q2, lambda_k2, subln_g, a_re, a_im,
    log_dt, b_re, b_im, c_re, c_im, d_skip, w_glu, b_glu, ssm_out_g, w_out, post_mix_g,
    pre_ffn_g, w_gate, w_up, w_down, post_ffn_g, pre_mix_gain_2, w_in_2, ln_v_gain_2,
    ln_v_bias_2, w_spatial_2, b_spatial_2, b_forget_2, out_norm_a_gain_2, out_norm_b_gain_2,
    w_out_2, post_mix_gain_2, pre_ffn_gain_2, w_ffn_in_2, w_ffn_out_2, post_ffn_gain_2,
):
    x = first_block(
        x, meta, pre_mix_g, w_in, lambda_q1, lambda_k1, lambda_q2, lambda_k2, subln_g, a_re,
        a_im, log_dt, b_re, b_im, c_re, c_im, d_skip, w_glu, b_glu, ssm_out_g, w_out,
        post_mix_g, pre_ffn_g, w_gate, w_up, w_down, post_ffn_g,
    )
    return second_block(
        x, pre_mix_gain_2, w_in_2, ln_v_gain_2, ln_v_bias_2, w_spatial_2, b_spatial_2,
        b_forget_2, out_norm_a_gain_2, out_norm_b_gain_2, w_out_2, post_mix_gain_2,
        pre_ffn_gain_2, w_ffn_in_2, w_ffn_out_2, post_ffn_gain_2,
    )


_drawn_inputs = setup_inputs


def setup_inputs(seed=0):
    import zlib

    import numpy as np

    out = dict(_drawn_inputs(seed))
    spreads = {}
    factors = {}
    for name, (base, spread) in spreads.items():
        noise = np.random.default_rng([zlib.crc32(name.encode()), seed]).standard_normal(out[name].shape)
        drawn = base * np.exp(spread * noise) if base else spread * noise
        out[name] = __import__('jax').numpy.asarray(drawn.astype(out[name].dtype))
    for name, factor in factors.items():
        out[name] = (out[name] * factor).astype(out[name].dtype)
    return out
```

```python
import math
from contextlib import ExitStack

import concourse.bass as bass
from concourse import mybir

F32 = mybir.dt.float32
F32R = mybir.dt.float32r
BF16 = mybir.dt.bfloat16
I32 = mybir.dt.int32
ALU = mybir.AluOpType
ACT = mybir.ActivationFunctionType
AX = mybir.AxisListType

P = 128
D = 1024
KT_D = D // P
SEQ = 1024
NT = SEQ // P
META = 16
L1 = SEQ + META
HALF = 512
D_FF = 2816
NF = D_FF // P
EPS = 1e-6
LN_EPS = 1e-5
TC = 8
NCH = L1 // TC
MCH = META // TC
GR = 32
HG = 16
ST = 64
GB = 4
NTAU = TC + 1
NSLOT = 12
NRAW = 4
NH1, NH2 = 4, 8
LAM_INIT = 0.8 - 0.6 * math.exp(-0.3 * 0)
NEG = -1.0e30
RSQRT_MAGIC = 0x5F3759DF

BASE = 16512
O_WH = 8192
O_WL = O_WH + NSLOT * 2048
O_RAW = O_WL + NSLOT * 2048
O_X = O_RAW + NRAW * 2048
O_H = O_X + 66560
O_FREE = O_H + 51456
O_END = 212832


def build(nc, io, stop=99):
    ctx = ExitStack()
    with ctx:
        _program(nc, io, ctx, stop)


def _program(nc, io, ctx, stop):
    ps = ctx.enter_context(nc.psum_tensor("ps", [P, 8, 512], F32))
    sems = {}

    def sem(name):
        if name not in sems:
            sems[name] = ctx.enter_context(nc.semaphore(name))
        return sems[name]

    def at(name, shape, dt, off):
        n = 2 if dt == BF16 else 4
        for s in shape[1:]:
            n *= s
        assert off + n <= O_END, (name, off, n)
        return nc.alloc_sbuf_tensor_at(name, shape, dt, offset=BASE + off)

    def bc(ap, axis, n):
        a = ap.unsqueeze(axis)
        shape = list(a.shape)
        shape[axis] = n
        return a.broadcast_to(shape)

    ident = at("ident", [P, P], F32, 0)
    identb = at("identb", [P, P], BF16, 512)
    maskb = at("maskb", [P, P], BF16, 768)
    rotT = at("rotT", [P, P], F32, 1024)
    ones = at("ones", [P, 8], F32, 1536)
    stat = at("stat", [P, 9, 8], F32, 1568)
    rst = at("rst", [P, 9, 8], F32, 1856)
    tmpa = at("tmpa", [P, 9, 8], F32, 2144)
    tmpb = at("tmpb", [P, 9, 8], F32, 2432)
    par = at("par", [P, 38, 32], F32, 3328)
    wh = at("wh", [P, NSLOT, 512], F32R, O_WH)
    wl = at("wl", [P, NSLOT, 512], F32R, O_WL)
    raw = at("raw", [P, NRAW, 512], F32, O_RAW)
    h_dram = [nc.dram_tensor(f"h{n}", (SEQ, D), F32, kind="Internal").ap() for n in range(3)]
    ud = nc.dram_tensor("ud", (HALF, TC, NCH), F32, kind="Internal").ap()
    yd = nc.dram_tensor("yd", (HALF, TC, NCH), F32, kind="Internal").ap()
    cd = nc.dram_tensor("cd", (NH2, SEQ), F32, kind="Internal").ap()

    def rows(ap, i):
        return ap[i * P:(i + 1) * P, :]

    met = sem("stage_met")
    count = {"n": 0}

    def meet(eng, k):
        eng.drain().then_inc(met, 1)
        eng.wait_ge(met, 3 * k)

    def chain(eng, name):
        s = sem(name)
        n = [0]

        def link(ins):
            n[0] += 1
            ins.then_inc(s, 1)
            eng.wait_ge(s, n[0])
        return link

    def rsqrt(v, link, x, out, a, b, scale, eps, factor=1.0):
        link(v.tensor_scalar(a, x, scale, eps, ALU.mult, ALU.add))
        link(v.tensor_scalar(b.bitcast(I32), a.bitcast(I32), 1, None, ALU.logical_shift_right))
        link(v.tensor_scalar(out.bitcast(I32), b.bitcast(I32), -1.0, float(RSQRT_MAGIC), ALU.mult, ALU.add))
        for n in range(3):
            link(v.tensor_tensor(b, out, out, ALU.mult))
            link(v.tensor_tensor(b, b, a, ALU.mult))
            link(v.tensor_scalar(b, b, -0.5, 1.5, ALU.mult, ALU.add))
            link(v.tensor_tensor(out, out, b, ALU.mult))
        if factor != 1.0:
            link(v.tensor_scalar(out, out, factor, None, ALU.mult))

    ROUND = 12582912.0
    LN2_HI, LN2_LO = 0.693359375, -2.12194440e-4

    def exact_exp(v, link, out, x, k, r):
        link(v.tensor_scalar(x, x, -87.0, 88.0, ALU.max, ALU.min))
        link(v.tensor_scalar(k, x, 1.4426950408889634, ROUND, ALU.mult, ALU.add))
        link(v.tensor_scalar(k, k, -ROUND, None, ALU.add))
        link(v.scalar_tensor_tensor(r, k, -LN2_HI, x, ALU.mult, ALU.add))
        link(v.scalar_tensor_tensor(r, k, -LN2_LO, r, ALU.mult, ALU.add))
        link(v.tensor_scalar(out, r, 1.0 / 5040, None, ALU.mult))
        for c in (1.0 / 720, 1.0 / 120, 1.0 / 24, 1.0 / 6, 0.5, 1.0):
            link(v.scalar_tensor_tensor(out, out, c, r, ALU.add, ALU.mult))
        link(v.tensor_scalar(out, out, 1.0, None, ALU.add))
        link(v.tensor_scalar(r.bitcast(I32), k, 127.0, None, ALU.add))
        link(v.tensor_scalar(r.bitcast(I32), r.bitcast(I32), 23, None, ALU.logical_shift_left))
        link(v.tensor_tensor(out, out, r, ALU.mult))

    stream = []

    def unit(dram, c0):
        n0 = len(stream)
        for k in range(dram.shape[0] // P):
            stream.append(dram[k * P:(k + 1) * P, c0:c0 + 512])
        return n0

    w_in = io["w_in"][0]
    w_in2 = io["w_in_2"][0]
    U_U, U_K, U_Q, U_V = (unit(w_in, c) for c in (1536, 512, 0, 1024))
    U_GLU = unit(io["w_glu"][0], 0)
    U_O1 = [unit(io["w_out"][0], c) for c in (0, 512)]
    N_BLOCK1 = len(stream)
    U_AV, U_AU, U_Q2, U_K2, U_V2 = (unit(w_in2, c) for c in (512, 0, 1024, 1536, 2048))
    U_O2 = [unit(io["w_out_2"][0], c) for c in (0, 512)]

    raw_in = [sem(f"raw_in{j}") for j in range(NRAW)]
    w_split, w_hi, w_free = sem("w_split"), sem("w_hi"), sem("w_free")

    def sp_weights(sp, n0, n1):
        for n in range(n0, n1):
            if n >= NRAW:
                sp.wait_ge(w_split, n - NRAW + 1)
            sp.dma_start(raw[:, n % NRAW, :], stream[n]).then_inc(raw_in[n % NRAW], 16)

    def pool_weights(pool, n0, n1):
        for n in range(n0, n1):
            pool.wait_ge(raw_in[n % NRAW], 16 * (n // NRAW + 1))
            if n >= NSLOT:
                pool.wait_ge(w_free, n - NSLOT + 1)
            s = n % NSLOT
            nc.gpsimd.tensor_copy(wh[:, s, :], raw[:, n % NRAW, :]).then_inc(w_hi, 1)
            pool.wait_ge(w_hi, n + 1)
            nc.gpsimd.tensor_tensor(wl[:, s, :], raw[:, n % NRAW, :], wh[:, s, :].bitcast(F32),
                                    ALU.subtract).then_inc(w_split, 1)

    def three(pe, out, lhs, rhs, first, last):
        pe.matmul(out, lhs[0], rhs[0], start=first, stop=False)
        pe.matmul(out, lhs[0], rhs[1], start=False, stop=False)
        return pe.matmul(out, lhs[1], rhs[0], start=False, stop=last)

    step_done = sem("step_done")
    emptied = [sem("emptied_by_vector"), sem("emptied_by_scalar")]
    steps = []

    def pe_step(pe, n, work):
        if n >= 2:
            pe.wait_ge(emptied[n % 2], n // 2)
        work(3 * (n % 2)).then_inc(step_done, 1)

    def chunks_of(c0, n):
        parts = -(-n // 512)
        size = -(-n // (parts * TC)) * TC
        return [(c0 + a, min(size, n - a)) for a in range(0, n, size)]

    def fm_work(pe, unit0, nk, m, x, c0, n):
        def work(bank):
            for k in range(nk):
                t = unit0 + k
                if m == 0:
                    pe.wait_ge(w_split, t + 1)
                s = t % NSLOT
                pair = (wh[:, s, m * P:(m + 1) * P], wl[:, s, m * P:(m + 1) * P])
                for j, (a, w) in enumerate(chunks_of(c0, n)):
                    mm = three(pe, ps[:, bank + j, 0:w], pair, (x[0][:, k, a:a + w], x[1][:, k, a:a + w]),
                               k == 0, k == nk - 1)
                if m == 3:
                    if k < nk - 1:
                        mm.then_inc(w_free, 1)
            if m == 3:
                pe.drain().then_inc(w_free, 1)
            return mm
        return work

    def tm_work(pe, unit0, nk, xs, c0, w, first, last):
        def work(bank):
            for k in range(nk):
                t = unit0 + k
                if first:
                    pe.wait_ge(w_split, t + 1)
                s = t % NSLOT
                xh, xl = xs[k]
                mm = three(pe, ps[0:w, bank, :], (xh[:, c0:c0 + w], xl[:, c0:c0 + w]),
                           (wh[:, s, :], wl[:, s, :]), k == 0, k == nk - 1)
                if last and k < nk - 1:
                    mm.then_inc(w_free, 1)
            if last:
                pe.drain().then_inc(w_free, 1)
            return mm
        return work

    class Turn:

        def __init__(self, tag, tiles, src, nseg, width, gain, xs, dst, cols, factor=1.0, w=None, turn=0):
            self.turn = turn
            self.tag, self.tiles, self.src, self.nseg, self.width = tag, tiles, src, nseg, width
            self.gain, self.xs, self.dst, self.cols, self.factor = gain, xs, dst, cols, factor
            self.w = w or (lambda i: P)
            self.nk = width // P
            self.scaled, self.turned = sem(tag + "_scaled"), sem(tag + "_turned")
            self.hi, self.lo, self.sq = sem(tag + "_hi"), sem(tag + "_lo"), sem(tag + "_sq")

        def n0(self):
            return self.turn * self.tiles * self.nk // 4

        def halves(self):
            for i in range(self.tiles):
                for b in range(0, self.nk, 4):
                    yield i, b

        def act(self, act, junk, before=None):
            for i in range(self.tiles):
                w, seg = self.w(i), self.width // self.nseg
                if before:
                    before(act, i)
                if i or self.turn:
                    act.wait_ge(self.sq, (self.turn * self.tiles + i) * self.nseg)
                for g in range(self.nseg):
                    nc.scalar.activation(junk[0:w, g * seg:(g + 1) * seg], self.src(i)[:, g * seg:(g + 1) * seg], ACT.Square,
                                         accum_out=stat[0:w, i, g:g + 1]).then_inc(self.sq, 1)
            n = 0
            for i, b in self.halves():
                act.wait_ge(self.turned, self.n0() + n + 1)
                w = self.w(i)
                src = ps[:, self.bank(n), 0:4 * w].rearrange("p (k c) -> p k c", k=4)
                nc.scalar.copy(self.dst(b, 0)[:, :, self.cols(i):self.cols(i) + w], src).then_inc(self.hi, 1)
                n += 1

        def bank(self, n):
            return n % 6

        def dve(self, v, link):
            v.wait_ge(self.sq, (self.turn + 1) * self.tiles * self.nseg)
            link(v.memset(tmpa[:, 0, 0:1], 0.0))
            cnt = self.tiles
            g = self.nseg
            rsqrt(v, link, stat[:, 0:cnt, 0:g], rst[:, 0:cnt, 0:g], tmpa[:, 0:cnt, 0:g], tmpb[:, 0:cnt, 0:g],
                  self.nseg / self.width, EPS, self.factor)
            seg = self.width // self.nseg
            per = self.nk // 4
            n = 0
            for i in range(self.tiles + 1):
                if i < self.tiles:
                    w = self.w(i)
                    if i >= 2:
                        v.wait_ge(self.turned, self.n0() + per * (i - 1))
                    for s in range(self.nseg):
                        c = slice(s * seg, (s + 1) * seg)
                        ins = v.scalar_tensor_tensor(self.xs[0:w, i % 2, c], self.src(i)[:, c],
                                                     rst[0:w, i, s:s + 1], self.gain[0:w, c], ALU.mult, ALU.mult)
                    ins.then_inc(self.scaled, 1)
                if i >= 1:
                    w = self.w(i - 1)
                    for b in range(0, self.nk, 4):
                        v.wait_ge(self.hi, self.n0() + n + 1)
                        cols = slice(self.cols(i - 1), self.cols(i - 1) + w)
                        v.tensor_tensor(self.dst(b, 1)[:, :, cols],
                                        ps[:, self.bank(n), 0:4 * w].rearrange("p (k c) -> p k c", k=4),
                                        self.dst(b, 0)[:, :, cols].bitcast(F32), ALU.subtract).then_inc(self.lo, 1)
                        n += 1

        def pe(self, pe):
            n = 0
            for i in range(self.tiles):
                w = self.w(i)
                pe.wait_ge(self.scaled, self.turn * self.tiles + i + 1)
                for b in range(0, self.nk, 4):
                    if n >= 6:
                        pe.wait_ge(self.lo, self.n0() + n - 5)
                    for k in range(4):
                        t = pe.transpose(ps[:, self.bank(n), k * w:(k + 1) * w],
                                         self.xs[0:w, i % 2, (b + k) * P:(b + k + 1) * P], ident[0:w, 0:w])
                    t.then_inc(self.turned, 1)
                    n += 1

    class Post:

        def __init__(self, turn, m, gain, res, res_dram, out_dram):
            self.turn, self.m, self.gain, self.res = turn, m, gain, res
            self.res_dram, self.out_dram = res_dram, out_dram
            self.res_in = [sem(f"post_res{j}") for j in range(2)]
            self.sq, self.normed, self.h = sem("post_sq"), sem("post_normed"), sem("post_h")

        def sp(self, sp):
            if stored[0]:
                sp.wait_ge(sem("stored"), stored[0])
            for i in range(NT + 2):
                if i < NT:
                    if i >= 2:
                        sp.wait_ge(self.h, self.turn * NT + i - 1)
                    sp.dma_start(self.res[:, i % 2, :], rows(self.res_dram, i)).then_inc(self.res_in[i % 2], 16)
                if i >= 2:
                    sp.wait_ge(self.h, self.turn * NT + i - 1)
                    sp.dma_start(rows(self.out_dram, i - 2), self.m[:, i - 2, :]).then_inc(sem("stored"), 16)
                    stored[0] += 16

        def act(self, act, junk):
            for i in range(NT):
                if i or self.turn:
                    act.wait_ge(self.sq, self.turn * NT + i)
                nc.scalar.activation(junk[:, 0:D], self.m[:, i, :], ACT.Square,
                                     accum_out=stat[:, i, 0:1]).then_inc(self.sq, 1)

        def dve(self, v, link):
            v.wait_ge(self.sq, (self.turn + 1) * NT)
            rsqrt(v, link, stat[:, 0:NT, 0:1], rst[:, 0:NT, 0:1], tmpa[:, 0:NT, 0:1], tmpb[:, 0:NT, 0:1],
                  1.0 / D, EPS)
            for i in range(NT + 1):
                if i < NT:
                    v.scalar_tensor_tensor(self.m[:, i, :], self.m[:, i, :], rst[:, i, 0:1], self.gain[:, 0:D],
                                           ALU.mult, ALU.mult).then_inc(self.normed, 1)
                if i >= 1:
                    v.wait_ge(self.normed, self.turn * NT + i)
                    v.wait_ge(self.res_in[(i - 1) % 2], 16 * (self.turn * NT // 2 + (i - 1) // 2 + 1))
                    v.tensor_tensor(self.m[:, i - 1, :], self.m[:, i - 1, :], self.res[:, (i - 1) % 2, :],
                                    ALU.add).then_inc(self.h, 1)

    stored = [0]
    loads = {}

    def load(eng, name, dst, src):
        loads[name] = loads.get(name, 0) + 16
        eng.dma_start(dst, src).then_inc(sem("in_" + name), 16)

    def loaded(eng, name, n=1):
        eng.wait_ge(sem("in_" + name), 16 * n)

    def rowb(ap):
        return ap.partition_broadcast(P)

    x_tok = at("x_tok", [P, 9, D], F32, O_H)
    xs1 = at("xs1", [P, 2, D], F32, O_H + 36864)
    gb1 = at("gb1", [P, D], F32, O_H + 45056)
    junk1 = at("junk1", [P, D], F32, O_FREE)
    x1h = at("x1h", [P, KT_D, L1], F32R, O_X)
    x1l = at("x1l", [P, KT_D, L1], F32R, O_X + 33280)
    q1 = at("q1", [P, 4, SEQ], F32, O_H)
    k1 = at("k1", [P, 4, L1], F32, O_H + 16384)
    v1 = at("v1", [P, 9, HALF], F32, O_H + 33024)
    ust = at("ust", [P, 2, TC, NCH], F32, O_FREE)
    rope_c = at("rope_c", [P, L1], F32, O_FREE + 8320)
    rope_s = at("rope_s", [P, L1], F32, O_FREE + 12480)
    rope_t = at("rope_t", [P, 2, 520], F32, O_FREE + 16640)

    def w1(i):
        return META if i == 0 else P

    def col1(i):
        return 0 if i == 0 else META + (i - 1) * P

    turn1 = Turn("turn1", 9, lambda i: x_tok[0:w1(i), i, :], 1, D, gb1, xs1,
                 lambda b, lo: (x1l if lo else x1h)[:, b:b + 4, :], col1, w=w1)

    n_steps = [0]
    plan1 = []
    for m in range(4):
        plan1.append(("u", U_U, m))
    for m in range(4):
        plan1.append(("k", U_K, m))
    for m in range(4):
        plan1.append(("q", U_Q, m))
    for i in range(9):
        plan1.append(("v", U_V, i))
    BASE1 = 0
    u_out = [sem("u_out0"), sem("u_out1")]

    def pe_plan(pe, plan, base, x, xk):
        for j, (kind, u0, m) in enumerate(plan):
            if kind in ("u", "k", "q", "q2", "k2"):
                c0, n = (META, SEQ) if kind == "q" else (0, SEQ) if kind in ("q2", "k2") else (0, L1)
                pe_step(pe, base + j, fm_work(pe, u0, 8, m, x, c0, n))
            elif kind == "v":
                pe_step(pe, base + j, tm_work(pe, u0, 8, xk, col1(m), w1(m), m == 0, m == 8))
            else:
                pe_step(pe, base + j, tm_work(pe, u0, 8, xk, m * P, P, m == 0, m == 7))

    x1k = [(x1h[:, k, :], x1l[:, k, :]) for k in range(KT_D)]

    def store_u(act, m):
        act.wait_ge(emptied[m % 2], m // 2 + 1)
        act.dma_start(ud[m * P:(m + 1) * P, :, :], ust[:, m % 2, :, :]).then_inc(u_out[m % 2], 16)

    def empty_plan1(eng, cp, parity):
        for j, (kind, u0, m) in enumerate(plan1):
            n = BASE1 + j
            if n % 2 != parity:
                continue
            eng.wait_ge(step_done, n + 1)
            bank = 3 * (n % 2)
            if kind == "u":
                if m >= 2:
                    eng.wait_ge(u_out[m % 2], 16)
                parts = chunks_of(0, L1)
                for c, (a, w) in enumerate(parts):
                    ins = cp(ust[:, m % 2, :, a // TC:(a + w) // TC].rearrange("p s c -> p c s"),
                             ps[:, bank + c, 0:w].rearrange("p (c s) -> p c s", s=TC), 1.0)
                    if c == len(parts) - 1:
                        ins.then_inc(emptied[parity], 1)
                if parity == 1:
                    store_u(eng, m - 1)
                    store_u(eng, m)
            elif kind in ("k", "q"):
                c0, tot, dst, scale = (0, L1, k1, 1.0) if kind == "k" else (META, SEQ, q1, ST ** -0.5)
                parts = chunks_of(c0, tot)
                for c, (a, w) in enumerate(parts):
                    ins = cp(dst[:, m, a - c0:a - c0 + w], ps[:, bank + c, 0:w], scale)
                ins.then_inc(emptied[parity], 1)
            else:
                w = w1(m)
                cp(v1[0:w, m, :], ps[0:w, bank, :], 1.0).then_inc(emptied[parity], 1)

    def act_cp(out, in_, scale):
        return nc.scalar.activation(out, in_, ACT.Copy, scale=scale)

    def dve_cp(out, in_, scale):
        return nc.vector.tensor_scalar(out, in_, scale, None, ALU.mult)

    rope_mm, rope_ts, rope_c1, rope_free = sem("rope_mm"), sem("rope_sin"), sem("rope_cos"), sem("rope_free")
    rope_jobs = []
    for dst, tot, c0 in ((k1, L1, 0), (q1, SEQ, META)):
        for m in range(4):
            for a, w in chunks_of(0, tot):
                rope_jobs.append((dst, m, a, w, c0 + a))

    def pe_rope(pe):
        for n, (t, m, a, w, pos) in enumerate(rope_jobs):
            if n >= 2:
                pe.wait_ge(rope_ts, n - 1)
            pe.matmul(ps[:, n % 2, 0:w], rotT[:, :], t[:, m, a:a + w], start=True, stop=True).then_inc(rope_mm, 1)

    def dve_rope(v, link):
        for n, (t, m, a, w, pos) in enumerate(rope_jobs):
            v.wait_ge(rope_mm, n + 1)
            v.tensor_tensor(rope_t[:, n % 2, 0:w], ps[:, n % 2, 0:w], rope_s[:, pos:pos + w], ALU.mult)\
                .then_inc(rope_ts, 1)
            v.tensor_tensor(t[:, m, a:a + w], t[:, m, a:a + w], rope_c[:, pos:pos + w], ALU.mult)\
                .then_inc(rope_c1, 1)
            v.wait_ge(rope_ts, n + 1)
            v.wait_ge(rope_c1, n + 1)
            v.tensor_tensor(t[:, m, a:a + w], t[:, m, a:a + w], rope_t[:, n % 2, 0:w], ALU.add)\
                .then_inc(rope_free, 1)

    us = at("us", [P, GR, NCH], F32, O_X)
    ctab = at("ctab", [P, GR, NCH], F32, O_X + 16640)
    stab = at("stab", [P, GR, NCH], F32, O_X + 33280)
    yb = at("yb", [P, 2, GB, NCH], F32, O_X + 49920)
    o = O_X + 54080
    fA = at("fA", [P, GB, NTAU, HG], F32, o); o += 2304
    fB = at("fB", [P, GB, NTAU, HG], F32, o); o += 2304
    eT = at("eT", [P, GB, TC, HG], F32, o); o += 2048
    eA = at("eA", [P, GB, P], F32, o); o += 2048
    eB = at("eB", [P, GB, P], F32, o); o += 2048
    assert o <= O_H
    o = O_FREE
    kst = at("kst", [P, GB, P], F32, o); o += 2048
    msb = at("msb", [P, 2, GB, P], F32, o); o += 4096
    cR = at("cR", [P, GR, HG], F32, o); o += 2048
    cI = at("cI", [P, GR, HG], F32, o); o += 2048
    bR = at("bR", [P, GR, HG], F32, o); o += 2048
    bI = at("bI", [P, GR, HG], F32, o); o += 2048
    bm = at("bm", [P, GR, HG], F32, o); o += 2048
    pA = at("pA", [P, GR, NTAU], F32, o); o += 1152
    pB = at("pB", [P, GR, NTAU], F32, o); o += 1152
    zin = at("zin", [P, GB, NCH], F32, o); o += 2080
    zc = at("zc", [P, GB, NCH], F32, o); o += 2080
    zs = at("zs", [P, GB, NCH], F32, o); o += 2080
    ftmp = at("ftmp", [P, GB, NTAU, HG], F32, o); o += 2304
    dsk = at("dsk", [HG, GR, HG], F32, o); o += 2048
    assert o <= O_END, o
    pR = at("pR", [P, GR, NTAU], F32, O_X + 54080)
    pI = at("pI", [P, GR, NTAU], F32, O_X + 55232)
    t5a = at("t5a", [P, GR, HG], F32, O_X + 56384)
    t5b = at("t5b", [P, GR, HG], F32, O_X + 58432)
    araw = at("araw", [GR, 2, 2, ST], F32, O_X + 60480)
    craw = at("craw", [P, 2, 4, 2, ST], F32, O_X + 61504)
    ddT = at("ddT", [HG, GR], F32, 2720)
    tab_t = at("tab_t", [P, GR, 64], F32, O_X)

    PN = {}

    def pv(name):
        if name not in PN:
            PN[name] = len(PN)
            assert len(PN) <= 38
        return par[:, PN[name], :]

    ssm_tr = sem("ssm_param_turned")
    c_jobs = [(r, t) for r in range(2) for t in range(4)]

    def sp_ssm_params(sp):
        for r, name in enumerate(("a_re", "a_im")):
            for dup in range(2):
                load(sp, "ssm_a", araw[:, r, dup, :], io[name][0])
        for r, name in enumerate(("c_re", "c_im")):
            for dup in range(2):
                load(sp, "ssm_c", craw[:, r, :, dup, :],
                     io[name][0].rearrange("g h p -> (g h) p").rearrange("(t q) p -> q t p", q=P))
        for r, (dst, name) in enumerate(((bR, "b_re"), (bI, "b_im"))):
            for dup in range(2):
                load(sp, "ssm_b", dst[dup * ST:(dup + 1) * ST, :, :], io[name][0].rearrange("g p h -> p g h"))
        load(sp, "ssm_dt", pv("dt"), rowb(io["log_dt"][0]))
        with nc.allow_non_contiguous_dma("a small transposed vector"):
            load(sp, "ssm_d", ddT[:, :], io["d_skip"][0].rearrange("(g h) -> h g", h=HG))

    def pe_ssm_params(pe):
        loaded(pe, "ssm_a", 4)
        for r in range(2):
            pe.transpose(ps[:, 0, r * GR:(r + 1) * GR], araw[:, r, :, :], ident[0:GR, 0:GR])
        loaded(pe, "ssm_c", 4)
        for r, t in c_jobs:
            tr = pe.transpose(ps[:, 1 + r, t * P:(t + 1) * P], craw[:, r, t, :, :], ident[:, :])
        tr.then_inc(ssm_tr, 1)

    def cmul(v, link, outr, outi, xr, xi, yr, yi, t1, t2):
        link(v.tensor_tensor(t1, xi, yi, ALU.mult))
        link(v.tensor_tensor(outr, xr, yr, ALU.mult))
        link(v.tensor_tensor(outr, outr, t1, ALU.subtract))
        link(v.tensor_tensor(t2, xi, yr, ALU.mult))
        link(v.tensor_tensor(outi, xr, yi, ALU.mult))
        link(v.tensor_tensor(outi, outi, t2, ALU.add))

    trig_in, trig_out = sem("trig_in"), sem("trig_out")
    TWO_PI_1, TWO_PI_2, TWO_PI_3 = 6.28125, 0.0019350051879882812, 3.0199159819e-07

    def act_ssm_params(act):
        act.wait_ge(trig_in, 1)
        nc.scalar.activation(pv("sin"), pv("rang"), ACT.Sin)
        nc.scalar.activation(pv("sinh"), pv("rang"), ACT.Sin, scale=0.5).then_inc(trig_out, 1)

    def dve_ssm_params(v, link):
        loaded(v, "ssm_dt")
        exact_exp(v, link, pv("edt"), pv("dt"), pv("k"), pv("r"))
        v.wait_ge(ssm_tr, 1)
        link(v.tensor_copy(pv("are"), ps[:, 0, 0:GR]))
        link(v.tensor_copy(pv("aim"), ps[:, 0, GR:2 * GR]))
        link(v.tensor_copy(cR[:, :, :].rearrange("p g h -> p (g h)"), ps[:, 1, :]))
        link(v.tensor_copy(cI[:, :, :].rearrange("p g h -> p (g h)"), ps[:, 2, :]))
        link(v.tensor_tensor(pv("ang"), pv("aim"), pv("edt"), ALU.mult))
        link(v.tensor_scalar(pv("k"), pv("ang"), 1.0 / (2 * math.pi), ROUND, ALU.mult, ALU.add))
        link(v.tensor_scalar(pv("k"), pv("k"), -ROUND, None, ALU.add))
        link(v.scalar_tensor_tensor(pv("rang"), pv("k"), -TWO_PI_1, pv("ang"), ALU.mult, ALU.add))
        link(v.scalar_tensor_tensor(pv("rang"), pv("k"), -TWO_PI_2, pv("rang"), ALU.mult, ALU.add))
        link(v.scalar_tensor_tensor(pv("rang"), pv("k"), -TWO_PI_3, pv("rang"), ALU.mult, ALU.add))
        link(v.tensor_scalar(pv("rang"), pv("rang"), -3.1415925, 3.1415925, ALU.max, ALU.min))
        v.tensor_copy(pv("k"), pv("rang")).then_inc(trig_in, 1)
        link(v.tensor_tensor(pv("x"), pv("are"), pv("edt"), ALU.mult))
        v.wait_ge(trig_in, 1)
        exact_exp(v, link, pv("mag"), pv("x"), pv("k"), pv("r"))
        v.wait_ge(trig_out, 1)
        link(v.tensor_tensor(pv("t1"), pv("sinh"), pv("sinh"), ALU.mult))
        link(v.tensor_scalar(pv("cos"), pv("t1"), -2.0, 1.0, ALU.mult, ALU.add))
        tau = lambda t, n: t[:, :, n]
        link(v.tensor_tensor(tau(pR, 1), pv("mag"), pv("cos"), ALU.mult))
        link(v.tensor_tensor(tau(pI, 1), pv("mag"), pv("sin"), ALU.mult))
        link(v.memset(tau(pR, 0), 1.0))
        link(v.memset(tau(pI, 0), 0.0))
        link(v.tensor_scalar(pv("nr"), tau(pR, 1), -1.0, None, ALU.add))
        link(v.tensor_tensor(pv("t1"), pv("are"), pv("are"), ALU.mult))
        link(v.tensor_tensor(pv("t2"), pv("aim"), pv("aim"), ALU.mult))
        link(v.tensor_tensor(pv("t1"), pv("t1"), pv("t2"), ALU.add))
        link(v.reciprocal(pv("rden"), pv("t1")))
        link(v.tensor_tensor(pv("t1"), pv("nr"), pv("are"), ALU.mult))
        link(v.tensor_tensor(pv("t2"), tau(pI, 1), pv("aim"), ALU.mult))
        link(v.tensor_tensor(pv("t1"), pv("t1"), pv("t2"), ALU.add))
        link(v.tensor_tensor(pv("fr"), pv("t1"), pv("rden"), ALU.mult))
        link(v.tensor_tensor(pv("t1"), tau(pI, 1), pv("are"), ALU.mult))
        link(v.tensor_tensor(pv("t2"), pv("nr"), pv("aim"), ALU.mult))
        link(v.tensor_tensor(pv("t1"), pv("t1"), pv("t2"), ALU.subtract))
        link(v.tensor_tensor(pv("fi"), pv("t1"), pv("rden"), ALU.mult))
        loaded(v, "ssm_b", 4)
        fr, fi = bc(pv("fr"), 2, HG), bc(pv("fi"), 2, HG)
        link(v.tensor_tensor(t5a[:, :, :], bR[:, :, :], fi, ALU.mult))
        link(v.tensor_tensor(t5b[:, :, :], bI[:, :, :], fi, ALU.mult))
        link(v.tensor_tensor(bR[:, :, :], bR[:, :, :], fr, ALU.mult))
        link(v.tensor_tensor(bI[:, :, :], bI[:, :, :], fr, ALU.mult))
        link(v.tensor_tensor(bR[:, :, :], bR[:, :, :], t5b[:, :, :], ALU.subtract))
        link(v.tensor_tensor(bI[:, :, :], bI[:, :, :], t5a[:, :, :], ALU.add))
        link(v.tensor_copy(bm[0:ST, :, :], bR[0:ST, :, :]))
        link(v.tensor_copy(bm[ST:P, :, :], bI[ST:P, :, :]))
        n = 1
        while n < TC:
            w = min(n, TC - n)
            yr, yi = bc(tau(pR, n), 2, w), bc(tau(pI, n), 2, w)
            a1, a2 = t5a[:, :, 0:w], t5b[:, :, 0:w]
            cmul(v, link, pR[:, :, n + 1:n + 1 + w], pI[:, :, n + 1:n + 1 + w],
                 pR[:, :, 1:1 + w], pI[:, :, 1:1 + w], yr, yi, a1, a2)
            n += w
        link(v.tensor_copy(pA[0:ST, :, :], pR[0:ST, :, :]))
        link(v.tensor_scalar(pA[ST:P, :, :], pI[ST:P, :, :], -1.0, None, ALU.mult))
        link(v.tensor_copy(pB[0:ST, :, :], pI[0:ST, :, :]))
        link(v.tensor_copy(pB[ST:P, :, :], pR[ST:P, :, :]))
        link(v.tensor_tensor(pv("m8"), pv("mag"), pv("mag"), ALU.mult))
        link(v.tensor_tensor(pv("m8"), pv("m8"), pv("m8"), ALU.mult))
        link(v.tensor_tensor(pv("m8"), pv("m8"), pv("m8"), ALU.mult))
        c, s = "cos", "sin"
        for n in (2, 4, 8):
            cmul(v, link, pv(f"c{n}"), pv(f"s{n}"), pv(c), pv(s), pv(c), pv(s), pv("t1"), pv("t2"))
            c, s = f"c{n}", f"s{n}"
        link(v.memset(ctab[:, :, 0], 1.0))
        link(v.memset(stab[:, :, 0], 0.0))
        link(v.tensor_copy(ctab[:, :, 1], pv("c8")))
        link(v.tensor_copy(stab[:, :, 1], pv("s8")))
        n = 1
        while n < NCH - 1:
            w = min(n, NCH - 1 - n)
            for a in range(0, w, 32):
                b = min(32, w - a)
                yr, yi = bc(ctab[:, :, n], 2, b), bc(stab[:, :, n], 2, b)
                cmul(v, link, ctab[:, :, n + 1 + a:n + 1 + a + b], stab[:, :, n + 1 + a:n + 1 + a + b],
                     ctab[:, :, 1 + a:1 + a + b], stab[:, :, 1 + a:1 + a + b], yr, yi,
                     tab_t[:, :, 0:b], tab_t[:, :, 32:32 + b])
            n += w
        loaded(v, "ssm_d")
        link(v.tensor_tensor(dsk[:, :, :], bc(ddT[:, :], 2, HG), bc(ident[0:HG, 0:HG], 1, GR), ALU.mult))
        link(v.memset(msb[:, :, :, :], 0.0))

    NB = GR // GB
    b_f = sem("ssm_rows_built")
    b_et = sem("ssm_in_rows_built")
    b_tr = sem("ssm_in_turned")
    b_k = sem("ssm_lags_done")
    b_kst = sem("ssm_lags_out")
    b_e = sem("ssm_in_ready")
    b_m = [sem("ssm_toeplitz0"), sem("ssm_toeplitz1")]
    b_s = sem("ssm_sums")
    b_z = sem("ssm_states_ready")
    b_y = sem("ssm_y_done")
    b_yc = sem("ssm_y_copied")
    b_yo = [sem("ssm_y_out0"), sem("ssm_y_out1")]
    yd_v = yd.rearrange("(g h) t c -> t h g c", h=HG)
    ud_v = ud.rearrange("(g h) s c -> s h g c", h=HG)

    def sp_ssm(sp):
        for n in range(NB):
            sp.wait_ge(b_kst, n + 1)
            if n >= 2:
                sp.wait_ge(b_y, n - 1)
            for s in range(TC):
                sp.dma_start(msb[(TC - 1 - s) * HG:(TC - s) * HG, n % 2, :, s * HG:P],
                             kst[0:HG, :, 0:P - s * HG]).then_inc(b_m[n % 2], 16)
            sp.wait_ge(b_yc, n + 1)
            for t in range(TC):
                sp.dma_start(yd_v[t, :, n * GB:(n + 1) * GB, :],
                             yb[t * HG:(t + 1) * HG, n % 2, :, :]).then_inc(b_yo[n % 2], 16)

    def dve_ssm(v, link):
        for n in range(NB):
            g = slice(n * GB, (n + 1) * GB)
            if n >= 1:
                v.wait_ge(b_y, n)
            cr, ci = (bc(t[:, g, :], 2, NTAU) for t in (cR, cI))
            a, b = (bc(t[:, g, :], 3, HG) for t in (pA, pB))
            br, bi = (bc(t[:, g, :], 2, TC) for t in (bR, bI))
            ae, be = (bc(t[:, g, 0:TC], 3, HG) for t in (pA, pB))
            ea = eA[:, :, :].rearrange("p g (t h) -> p g t h", h=HG)
            v.tensor_tensor(fA[:, :, :, :], cr, a, ALU.mult)
            link(v.tensor_tensor(ftmp[:, :, :, :], ci, b, ALU.mult))
            link(v.tensor_tensor(fA[:, :, :, :], fA[:, :, :, :], ftmp[:, :, :, :], ALU.subtract))
            v.tensor_tensor(fB[:, :, :, :], cr, b, ALU.mult)
            link(v.tensor_tensor(ftmp[:, :, :, :], ci, a, ALU.mult))
            fb, ft = (t[:, :, :, :].rearrange("p g t h -> p (g t h)") for t in (fB, ftmp))
            link(v.scalar_tensor_tensor(fb, fb, -1.0, ft, ALU.mult, ALU.subtract))
            v.tensor_tensor(eT[:, :, :, :], bi, be, ALU.mult)
            link(v.tensor_tensor(ea, br, ae, ALU.mult))
            ins = v.tensor_tensor(eT[:, :, :, :], ea, eT[:, :, :, :], ALU.subtract)
            ins.then_inc(b_et, 1)
            v.wait_ge(b_k, n + 1)
            if n >= 1:
                v.wait_ge(b_m[(n - 1) % 2], 128 * ((n - 1) // 2 + 1))
            link(v.tensor_copy(kst[0:HG, :, HG:P], ps[0:HG, 0, :].rearrange("p (g c) -> p g c", g=GB)[:, :, HG:P]))
            v.tensor_tensor(kst[0:HG, :, 0:HG], ps[0:HG, 0, :].rearrange("p (g c) -> p g c", g=GB)[:, :, 0:HG],
                            dsk[:, g, :], ALU.add).then_inc(b_kst, 1)
            tr = ps[:, 1, :].rearrange("p (g c) -> p g c", g=GB)
            v.tensor_copy(eA[:, :, 0:ST], tr[:, :, 0:ST])
            v.tensor_scalar(eA[:, :, ST:P], tr[:, :, ST:P], -1.0, None, ALU.mult)
            v.tensor_scalar(eB[:, :, 0:ST], tr[:, :, ST:P], -1.0, None, ALU.mult)
            v.tensor_scalar(eB[:, :, ST:P], tr[:, :, 0:ST], -1.0, None, ALU.mult).then_inc(b_e, 1)
            v.wait_ge(b_s, n + 1)
            for h in range(2):
                gg = slice(n * GB + 2 * h, n * GB + 2 * h + 2)
                jj = slice(2 * h, 2 * h + 2)
                sa = ps[:, 2 + h, 0:2 * NCH].rearrange("p (g c) -> p g c", g=2)[:, :, 0:NCH - 1]
                sb = ps[:, 4 + h, 0:2 * NCH].rearrange("p (g c) -> p g c", g=2)[:, :, 0:NCH - 1]
                v.tensor_tensor(zin[:, jj, 1:NCH], sa, ctab[:, gg, 1:NCH], ALU.mult)
                link(v.tensor_tensor(zs[:, jj, 1:NCH], sb, stab[:, gg, 1:NCH], ALU.mult))
                link(v.tensor_tensor(zin[:, jj, 1:NCH], zin[:, jj, 1:NCH], zs[:, jj, 1:NCH], ALU.add))
            v.memset(zc[:, :, 0:1], 0.0)
            for j in range(GB):
                gi = n * GB + j
                ins = v.tensor_tensor_scan(zc[:, j, 1:NCH], pv("m8")[:, gi:gi + 1].broadcast_to([P, NCH - 1]),
                                           zin[:, j, 1:NCH], 0.0, ALU.mult, ALU.add)
                link(ins)
            link(v.tensor_tensor(zs[:, :, :], zc[:, :, :], stab[:, g, :], ALU.mult))
            v.tensor_tensor(zc[:, :, :], zc[:, :, :], ctab[:, g, :], ALU.mult).then_inc(b_z, 1)

    def act_ssm(act):
        for n in range(NB):
            act.wait_ge(b_y, n + 1)
            if n >= 2:
                act.wait_ge(b_yo[n % 2], 128 * (n // 2))
            for h in range(2):
                ins = nc.scalar.copy(yb[:, n % 2, 2 * h:2 * h + 2, :],
                                     ps[:, 6 + h, 0:2 * NCH].rearrange("p (g c) -> p g c", g=2))
            ins.then_inc(b_yc, 1)

    def pe_ssm(pe):
        loaded(pe, "us", TC)
        for n in range(NB):
            pe.wait_ge(b_et, n + 1)
            for j in range(GB):
                pe.transpose(ps[:, 1, j * P:(j + 1) * P], eT[:, j], ident[:, :])
            for j in range(GB):
                mm = pe.matmul(ps[0:HG, 0, j * P:(j + 1) * P], bm[:, n * GB + j, :],
                               fA[:, j, 0:TC, :], start=True, stop=True)
            mm.then_inc(b_k, 1)
            pe.wait_ge(b_e, n + 1)
            for which, src in ((2, eA), (4, eB)):
                for j in range(GB):
                    mm = pe.matmul(ps[:, which + j // 2, (j % 2) * NCH:(j % 2 + 1) * NCH], src[:, j, :],
                                   us[:, n * GB + j, :], start=True, stop=True)
            mm.then_inc(b_s, 1)
            pe.wait_ge(b_z, n + 1)
            pe.wait_ge(b_m[n % 2], 128 * (n // 2 + 1))
            if n >= 1:
                pe.wait_ge(b_yc, n)
            for j in range(GB):
                out = ps[:, 6 + j // 2, (j % 2) * NCH:(j % 2 + 1) * NCH]
                pe.matmul(out, msb[:, n % 2, j, :], us[:, n * GB + j, :], start=True, stop=False)
                pe.matmul(out, fA[:, j, 1:NTAU, :], zc[:, j, :], start=False, stop=False)
                mm = pe.matmul(out, fB[:, j, 1:NTAU, :], zs[:, j, :], start=False, stop=True)
            mm.then_inc(b_y, 1)


    def load_us(eng):
        for j in range(2):
            eng.wait_ge(u_out[j], 32)
        for s in range(TC):
            load(eng, "us", us[(TC - 1 - s) * HG:(TC - s) * HG, :, :], ud_v[s])

    class Attention:

        def __init__(self, tag, q, k, v, out, heads, dv, meta, maps, ex, atb, bias=None, neglam=None):
            self.tag, self.q, self.k, self.v, self.out = tag, q, k, v, out
            self.heads, self.dv, self.meta, self.maps = heads, dv, meta, maps
            self.ex, self.atb, self.bias, self.neglam = ex, atb, bias, neglam
            self.items = [(h, i) for h in range(heads) for i in range(NT)]
            names = ("s0", "s1", "max0", "max1", "exp0", "exp1", "prob", "turned", "evac0", "evac1", "pv",
                     "o_out")
            self.s = {n: sem(f"{tag}_{n}") for n in names if maps == 2 or n not in ("s1", "max1", "exp1")}
            self.batches = []
            for n, (h, i) in enumerate(self.items):
                full = [(meta + t * P, P, t + (1 if meta else 0)) for t in range(i + 1)]
                tiles = full + ([(0, meta, 0)] if meta else [])
                for b in range(0, len(tiles), 4):
                    self.batches.append((n, tiles[b:b + 4]))
            self.first = {}
            for b, (n, _) in enumerate(self.batches):
                self.first.setdefault(n, b)
            self.first[len(self.items)] = len(self.batches)
            self.beside_long = {b for n in range(len(self.items)) if self.items[n][1] == NT - 3
                                for b in self.steps(n)}

        def ncols(self, i):
            return self.meta + (i + 1) * P

        def base(self, n, m):
            return 3 * m if self.maps == 2 else 2 * (n % 2)

        def score(self, n, m, c0, c1):
            b = self.base(n, m)
            return ps[:, b:b + (3 if self.maps == 2 else 2), :].rearrange("p b c -> p (b c)")[:, c0:c1]

        def obank(self, n):
            if self.maps == 2:
                return ps[:, 5 + 2 * (n % 2), 0:self.dv]
            return ps[:, 4 + n % 2, 0:self.dv]

        def tbank(self, b):
            if self.maps == 2:
                return 6 if b % 2 == 0 or b in self.beside_long else 2
            return 6 + b % 2

        def bank_free(self, pe, bank, b):
            last = [p for p in range(max(b, 0)) if self.tbank(p) == bank]
            if last:
                pe.wait_ge(self.s[f"evac{last[-1] % 2}"], last[-1] // 2 + 1)

        def steps(self, n):
            return range(self.first[n] + 1, min(self.first[n + 1] + 1, len(self.batches)))

        def pe_scores(self, pe, n):
            h, i = self.items[n]
            w = self.ncols(i)
            if w > SEQ:
                pe.wait_ge(self.s["o_out"], n - 2)
                self.bank_free(pe, 2, self.first[n - 2] + 1)
            for m in range(self.maps):
                if self.maps == 2 and n >= 1:
                    pe.wait_ge(self.s[f"exp{m}"], n)
                if self.maps == 1 and n >= 2:
                    pe.wait_ge(self.s["max0"], n - 1)
                t, r = m * self.heads // 2 + h // 2, 64 * (h % 2)
                for a in range(0, w, 512):
                    b = min(a + 512, w)
                    d0 = max(a, w - P)
                    mm = pe.matmul(self.score(n, m, a, b), self.q[r:r + 64, t, i * P:(i + 1) * P],
                                   self.k[r:r + 64, t, a:b], start=True, stop=True)
                    if d0 < b:
                        mm = pe.matmul(self.score(n, m, d0, b), identb[:, :], maskb[:, d0 - (w - P):b - (w - P)],
                                       start=False, stop=True, skip_group_check=True)
                mm.then_inc(self.s[f"s{m}"], 1)

        def pe_turn(self, pe, b):
            n, tiles = self.batches[b]
            if b == self.first[n]:
                pe.wait_ge(self.s["prob" if self.maps == 2 else "exp0"], n + 1)
            self.bank_free(pe, self.tbank(b), b)
            for j, (c, w, _) in enumerate(tiles):
                t = pe.transpose(ps[0:w, self.tbank(b), j * P:(j + 1) * P], self.ex[:, n % 3, 0, c:c + w],
                                 ident[:, :])
            t.then_inc(self.s["turned"], 1)

        def pe_pv(self, pe, b):
            n, tiles = self.batches[b]
            h, i = self.items[n]
            if b == self.first[n] and n >= 2:
                pe.wait_ge(self.s["o_out"], n - 1)
            if b == self.first[n] and self.maps == 2 and i == NT - 2:
                pe.wait_ge(self.s["exp1"], n + 2)
            pe.wait_ge(self.s[f"evac{b % 2}"], b // 2 + 1)
            for j, (c, w, t) in enumerate(tiles):
                first, last = b == self.first[n] and j == 0, b == self.first[n + 1] - 1 and j == len(tiles) - 1
                mm = pe.matmul(self.obank(n), self.atb[0:w, b % 3, j, :], self.v[0:w, t, h * self.dv:(h + 1) * self.dv],
                               start=first, stop=last, skip_group_check=True)
            mm.then_inc(self.s["pv"], 1)


        def pe(self, pe):
            self.pe_scores(pe, 0)
            self.pe_scores(pe, 1)
            self.pe_turn(pe, 0)
            for n in range(len(self.items)):
                if n + 2 < len(self.items):
                    self.pe_scores(pe, n + 2)
                for b in range(self.first[n], self.first[n + 1]):
                    if b + 1 < len(self.batches):
                        self.pe_turn(pe, b + 1)
                    self.pe_pv(pe, b)

        def evacuate(self, eng, cp, b):
            n, tiles = self.batches[b]
            eng.wait_ge(self.s["turned"], b + 1)
            if b >= 3:
                eng.wait_ge(self.s["pv"], b - 2)
            full = [t for t in tiles if t[1] == P]
            if full:
                ins = cp(self.atb[:, b % 3, 0:len(full), :],
                         ps[:, self.tbank(b), 0:len(full) * P].rearrange("p (t q) -> p t q", q=P))
            if len(full) < len(tiles):
                j, w = len(full), tiles[-1][1]
                ins = cp(self.atb[0:w, b % 3, j, :], ps[0:w, self.tbank(b), j * P:(j + 1) * P])
            ins.then_inc(self.s[f"evac{b % 2}"], 1)

        def act_exp(self, act, n):
            w = self.ncols(self.items[n][1])
            if n >= 3:
                act.wait_ge(self.s["turned"], self.first[n - 2])
            for m in range(self.maps):
                act.wait_ge(self.s[f"max{m}"], n + 1)
                src = self.score(n, m, 0, w) if self.maps == 2 else self.ex[:, n % 3, 0, 0:w]
                nc.scalar.activation(self.ex[:, n % 3, m, 0:w], src, ACT.Exp, bias=negmax[:, n % 3, m:m + 1],
                                     accum_out=psum_l[:, n % 3, m:m + 1]).then_inc(self.s[f"exp{m}"], 1)

        def act(self, act):
            self.act_exp(act, 0)
            self.act_exp(act, 1)
            if self.maps == 2:
                self.evacuate(act, nc.scalar.copy, 0)
            for n in range(len(self.items)):
                for b in self.steps(n):
                    if self.maps == 2 or b % 2 == 1:
                        self.evacuate(act, nc.scalar.copy, b)
                if n + 2 < len(self.items):
                    self.act_exp(act, n + 2)

        def dve_max(self, v, n, link):
            w = self.ncols(self.items[n][1])
            h = self.items[n][0]
            for m in range(self.maps):
                v.wait_ge(self.s[f"s{m}"], n + 1)
                if n >= 3:
                    v.wait_ge(self.s[f"exp{m}"], n - 2)
                if self.maps == 2:
                    v.tensor_reduce(negmax[:, n % 3, m:m + 1], self.score(n, m, 0, w), AX.X, ALU.max,
                                    negate=True).then_inc(self.s[f"max{m}"], 1)
                else:
                    if n >= 3:
                        v.wait_ge(self.s["turned"], self.first[n - 2])
                    link(v.tensor_tensor_reduce(self.ex[:, n % 3, 0, 0:w], self.score(n, 0, 0, w),
                                                self.bias[:, h, 0:w], 1.0, -3.0e38, ALU.add, ALU.max,
                                                lmax[:, n % 2, 0:1]))
                    v.tensor_scalar(negmax[:, n % 3, 0:1], lmax[:, n % 2, 0:1], -1.0, None, ALU.mult)\
                        .then_inc(self.s["max0"], 1)

        def dve_prob(self, v, n, link):
            w = self.ncols(self.items[n][1])
            for m in range(2):
                v.wait_ge(self.s[f"exp{m}"], n + 1)
            link(v.reciprocal(rl[:, n % 3, 0:2], psum_l[:, n % 3, 0:2]))
            link(v.tensor_scalar(rho[:, n % 3, 0:1], psum_l[:, n % 3, 0:1], rl[:, n % 3, 1:2], self.neglam,
                                 ALU.mult, ALU.mult))
            v.scalar_tensor_tensor(self.ex[:, n % 3, 0, 0:w], self.ex[:, n % 3, 1, 0:w], rho[:, n % 3, 0:1],
                                   self.ex[:, n % 3, 0, 0:w], ALU.mult, ALU.add).then_inc(self.s["prob"], 1)

        def dve_out(self, v, n, link):
            h, i = self.items[n]
            if self.maps == 1:
                v.wait_ge(self.s["exp0"], n + 1)
                link(v.reciprocal(rl[:, n % 3, 0:1], psum_l[:, n % 3, 0:1]))
            v.wait_ge(self.s["pv"], self.first[n + 1])
            v.tensor_scalar(self.out[:, i, h * self.dv:(h + 1) * self.dv], self.obank(n), rl[:, n % 3, 0:1],
                            None, ALU.mult).then_inc(self.s["o_out"], 1)

        def dve(self, v, link):
            N = len(self.items)
            self.dve_max(v, 0, link)
            self.dve_max(v, 1, link)
            if self.maps == 2:
                self.dve_prob(v, 0, link)
            else:
                self.evacuate(v, nc.vector.tensor_copy, 0)
            for n in range(N):
                if self.maps == 2 and n + 1 < N:
                    self.dve_prob(v, n + 1, link)
                if n + 2 < N:
                    self.dve_max(v, n + 2, link)
                for b in self.steps(n):
                    if self.maps == 1 and b % 2 == 0:
                        self.evacuate(v, nc.vector.tensor_copy, b)
                self.dve_out(v, n, link)

    negmax = at("negmax", [P, 3, 2], F32, 2848)
    lmax = at("lmax", [P, 2, 2], F32, 2880)
    psum_l = at("psum_l", [P, 3, 2], F32, 2912)
    rl = at("rl", [P, 3, 2], F32, 2944)
    rho = at("rho", [P, 3, 2], F32, 2976)
    lamv = at("lamv", [P, 8], F32, 3008)

    class Mlp:

        def __init__(self, tag, turn, wg, wu, wd, x, acc):
            self.tag, self.turn, self.x, self.acc = tag, turn, x, acc
            self.wg, self.wu = (w.rearrange("(k p) (f c) -> p f k c", p=P, c=P) for w in (wg, wu))
            self.wd = wd.rearrange("(f p) n -> p f n", p=P)
            names = ("raw0", "raw1", "raw2", "ready0", "ready1", "ready2", "hi0", "hi1", "hi2", "gate", "up",
                     "down", "silu", "prod", "f_hi", "f_lo", "added")
            self.s = {n: sem(f"mlp_{n}") for n in names}
            self.total = {"down": 2 * NT + NT * NF, "added": 2 + NT * NF, "f_hi": NF, "f_lo": NF}
            for n in ("silu", "prod", "ready0", "ready1", "ready2"):
                self.total[n] = 1 + NF
            for n in ("gate", "up"):
                self.total[n] = 2 + NF
            for j in range(3):
                self.total[f"hi{j}"], self.total[f"raw{j}"] = NF, 16 * NF
            o = O_WH
            self.sh = [at(f"{tag}_w{j}h", [P, 2, D], F32R, O_WH + j * 16384) for j in range(3)]
            self.sl = [at(f"{tag}_w{j}l", [P, 2, D], F32R, O_WH + j * 16384 + 8192) for j in range(3)]
            o = O_H + 32768
            self.raw = at(f"{tag}_raw", [P, 3, D], F32, o); o += 12288
            self.fh = at(f"{tag}_fh", [P, 2, SEQ], F32R, o); o += 8192
            self.fl = at(f"{tag}_fl", [P, 2, SEQ], F32R, o); o += 8192
            self.sil = at(f"{tag}_sil", [P, SEQ], F32, o); o += 4096
            self.f = at(f"{tag}_f", [P, SEQ], F32, o)

        def wait(self, eng, name, value):
            eng.wait_ge(self.s[name], value + self.turn * self.total[name])

        def sp(self, sp):
            with sp.Fori(0, NF // 2) as it:
                for b in range(2):
                    f = it * 2 + b
                    for j, src in enumerate((self.wg, self.wu)):
                        self.wait(sp, f"ready{j}", f + 1)
                        sp.dma_start(self.raw[:, j, :].rearrange("p (k c) -> p k c", k=KT_D),
                                     src[:, bass.ds(f, 1), :, :].rearrange("p f k c -> p (f k) c"))\
                            .then_inc(self.s[f"raw{j}"], 16)
                    self.wait(sp, "ready2", f + 1)
                    sp.dma_start(self.raw[:, 2, :], self.wd[:, bass.ds(f, 1), :].rearrange("p f n -> p (f n)"))\
                        .then_inc(self.s["raw2"], 16)

        def pool(self, pool):
            for j in range(3):
                pool.sem_inc(self.s[f"ready{j}"], 1)
            with pool.Fori(0, NF // 2) as it:
                for b in range(2):
                    f = it * 2 + b
                    for j, (used, per) in enumerate((("gate", 1), ("up", 1), ("down", NT))):
                        self.wait(pool, f"raw{j}", 16 * (f + 1))
                        self.wait(pool, used, per * (f + 1))
                        nc.gpsimd.tensor_tensor(self.sh[j][:, b, :], self.raw[:, j, :],
                                                ones[:, 0:1].broadcast_to([P, D]), ALU.mult)\
                            .then_inc(self.s[f"hi{j}"], 1)
                        self.wait(pool, f"hi{j}", f + 1)
                        nc.gpsimd.tensor_tensor(self.sl[j][:, b, :], self.raw[:, j, :],
                                                self.sh[j][:, b, :].bitcast(F32), ALU.subtract)\
                            .then_inc(self.s[f"ready{j}"], 1)

        def pe_in(self, pe, f, b, j, name, freed):
            self.wait(pe, f"ready{j}", f + 2)
            self.wait(pe, freed, f + 1)
            for k in range(KT_D):
                w = (self.sh[j][:, b, k * P:(k + 1) * P], self.sl[j][:, b, k * P:(k + 1) * P])
                for h in range(2):
                    c = slice(h * HALF, (h + 1) * HALF)
                    mm = three(pe, ps[:, 2 * j + h, :], w, (self.x[0][:, k, c], self.x[1][:, k, c]),
                               k == 0, k == KT_D - 1)
            mm.then_inc(self.s[name], 1)

        def pe_down(self, pe, f, b):
            self.wait(pe, "ready2", f + 2)
            self.wait(pe, "f_lo", f + 1)
            for i in range(NT):
                self.wait(pe, "added", NT * f + i + 1)
                c = slice(i * P, (i + 1) * P)
                for h in range(2):
                    n = slice(h * HALF, (h + 1) * HALF)
                    mm = three(pe, ps[:, 4 + 2 * (i % 2) + h, :], (self.fh[:, b, c], self.fl[:, b, c]),
                               (self.sh[2][:, b, n], self.sl[2][:, b, n]), True, True)
                mm.then_inc(self.s["down"], 1)

        def pe(self, pe):
            for name, n in (("gate", 2), ("up", 2), ("down", 2 * NT)):
                pe.sem_inc(self.s[name], n)
            self.pe_in(pe, 0, 0, 0, "gate", "silu")
            self.pe_in(pe, 0, 0, 1, "up", "prod")
            with pe.Fori(0, NF // 2 - 1) as it:
                for b in range(2):
                    f = it * 2 + b
                    self.pe_in(pe, f + 1, 1 - b, 0, "gate", "silu")
                    self.pe_in(pe, f + 1, 1 - b, 1, "up", "prod")
                    self.pe_down(pe, f, b)
            self.pe_in(pe, NF - 1, 1, 0, "gate", "silu")
            self.pe_in(pe, NF - 1, 1, 1, "up", "prod")
            self.pe_down(pe, NF - 2, 0)
            self.pe_down(pe, NF - 1, 1)

        def act(self, act):
            act.sem_inc(self.s["silu"], 1)
            with act.Fori(0, NF // 2) as it:
                for b in range(2):
                    f = it * 2 + b
                    self.wait(act, "gate", f + 3)
                    self.wait(act, "prod", f + 1)
                    nc.scalar.activation(self.sil[:, :], ps[:, 0:2, :].rearrange("p b c -> p (b c)"), ACT.Silu)\
                        .then_inc(self.s["silu"], 1)
                    self.wait(act, "prod", f + 2)
                    self.wait(act, "down", NT * (f + 1))
                    nc.scalar.copy(self.fh[:, b, :], self.f[:, :]).then_inc(self.s["f_hi"], 1)

        def dve_hidden(self, v, f, b):
            if not isinstance(f, int) or f:
                self.wait(v, "f_lo", f)
            self.wait(v, "up", f + 3)
            self.wait(v, "silu", f + 2)
            v.tensor_tensor(self.f[:, :], self.sil[:, :], ps[:, 2:4, :].rearrange("p b c -> p (b c)"),
                            ALU.mult).then_inc(self.s["prod"], 1)
            self.wait(v, "f_hi", f + 1)
            v.tensor_tensor(self.fl[:, b, :], self.f[:, :], self.fh[:, b, :].bitcast(F32), ALU.subtract)\
                .then_inc(self.s["f_lo"], 1)

        def dve_add(self, v, f):
            for i in range(NT):
                self.wait(v, "down", NT * f + i + 1 + 2 * NT)
                b = 4 + 2 * (i % 2)
                v.tensor_tensor(self.acc[:, i, :], self.acc[:, i, :],
                                ps[:, b:b + 2, :].rearrange("p b c -> p (b c)"), ALU.add)\
                    .then_inc(self.s["added"], 1)

        def dve(self, v, link):
            v.sem_inc(self.s["prod"], 1)
            v.sem_inc(self.s["added"], 2)
            v.wait_ge(sem("stored"), 16 * NT * (1 + 2 * self.turn))
            link(v.memset(self.acc[:, :, :], 0.0))
            self.dve_hidden(v, 0, 0)
            with v.Fori(0, NF // 2 - 1) as it:
                for b in range(2):
                    f = it * 2 + b
                    self.dve_add(v, f)
                    self.dve_hidden(v, f + 1, 1 - b)
            self.dve_add(v, NF - 2)
            self.dve_hidden(v, NF - 1, 1)
            self.dve_add(v, NF - 1)

    o1 = at("o1", [P, NT, HALF], F32, O_X)
    ex1 = at("ex1", [P, 3, 2, L1], F32, O_X + 16384)
    at1 = at("at1", [P, 3, 4, P], F32, O_X + 41344)
    yg = at("yg", [P, 4, TC, NCH], F32, O_FREE)
    att1 = Attention("att1", q1, k1, v1, o1, NH1, P, META, 2, ex1, at1, neglam=lamv[:, 4:5])
    oth = at("oth", [P, 4, SEQ], F32R, O_X + 32768)
    otl = at("otl", [P, 4, SEQ], F32R, O_X + 49152)
    gyh = at("gyh", [P, 4, SEQ], F32R, O_X)
    gyl = at("gyl", [P, 4, SEQ], F32R, O_X + 16384)
    gy = at("gy", [P, 4, SEQ], F32, O_H)
    sig = at("sig", [P, 2, SEQ], F32, O_H + 16384)
    ysq = at("ysq", [P, 4, SEQ], F32, O_FREE)
    o = O_H + 32768
    xs_b = at("xs_b", [P, 2, D], F32, o); o += 8192
    gb_b = at("gb_b", [P, D], F32, o); o += 4096
    gb_c = at("gb_c", [P, D], F32, o); o += 4096
    junk_b = at("junk_b", [P, D], F32, o); o += 4096
    res_b = at("res_b", [P, 2, D], F32, o); o += 8192
    hbuf = at("hbuf", [P, NT, D], F32, O_H)
    bcol = at("bcol", [P, 8], F32, 3040)
    sgcol = at("sgcol", [P, 4], F32, 3072)
    xs_o = at("xs_o", [P, 2, HALF], F32, O_H)
    gb_o = at("gb_o", [P, HALF], F32, O_H + 4096)
    junk_o = at("junk_o", [P, HALF], F32, O_H + 6144)
    turn_o = Turn("turn_o", NT, lambda i: o1[:, i, :], NH1, HALF, gb_o, xs_o,
                  lambda b, lo: (otl if lo else oth)[:, b:b + 4, :], lambda i: i * P, factor=1.0 - LAM_INIT)
    xh = at("xh", [P, KT_D, SEQ], F32R, O_X)
    xl = at("xl", [P, KT_D, SEQ], F32R, O_X + 32768)
    xdst = lambda b, lo: (xl if lo else xh)[:, b:b + 4, :]
    hsrc = lambda i: hbuf[:, i, :]
    post = [None] * 4
    turn_h = [None] * 3
    res_of = [io["x"][0], h_dram[0], h_dram[1], h_dram[2]]
    out_of = [h_dram[0], h_dram[1], h_dram[2], io["out"][0]]
    for n in range(4):
        post[n] = Post(n, hbuf, gb_b, res_b, res_of[n], out_of[n])
        if n < 3:
            turn_h[n] = Turn("turn_h", NT, hsrc, 1, D, gb_c, xs_b, xdst, lambda i: i * P, turn=n)
    post_gain = [io["post_mix_g"][0], io["post_ffn_g"][0], io["post_mix_gain_2"][0], io["post_ffn_gain_2"][0]]
    turn_gain = [io["pre_ffn_g"][0], io["pre_mix_gain_2"][0], io["pre_ffn_gain_2"][0]]
    mlp1 = Mlp("mlp1", 0, io["w_gate"][0], io["w_up"][0], io["w_down"][0], (xh, xl), hbuf)
    wf2 = io["w_ffn_in_2"][0]
    mlp2 = Mlp("mlp2", 1, wf2[:, 0:D_FF], wf2[:, D_FF:2 * D_FF], io["w_ffn_out_2"][0], (xh, xl), hbuf)
    av = at("av", [P, NT, HALF], F32, O_H)
    v2 = av
    au = at("au", [P, NT, HALF], F32, O_H + 16384)
    q2 = at("q2", [P, 4, SEQ], F32, O_H + 32768)
    k2 = at("k2", [P, 4, SEQ], F32, O_H + 49152)
    wfh = at("wfh", [P, KT_D, P], F32R, O_H + 32768)
    wfl = at("wfl", [P, KT_D, P], F32R, O_H + 36864)
    wfp = at("wfp", [P, KT_D, P], F32, O_H + 40960)
    wfr = at("wfr", [P, KT_D, NH2], F32, O_H + 45056)
    o = O_H + 65536
    lng = at("lng", [P, HALF], F32, o); o += 2048
    lnb = at("lnb", [P, HALF], F32, o); o += 2048
    wsT = at("wsT", [P, 8, P], F32, o); o += 4096
    fl_a = at("fl_a", [NH2, SEQ], F32, o)
    wsp = at("wsp", [P, 8, P], F32, O_H + 49152)
    fl_b = at("fl_b", [NH2, SEQ], F32, O_H + 53248)
    fl_c = at("fl_c", [NH2, SEQ], F32, O_H + 57344)
    bn = at("bn", [P, NT, 8], F32, 3104 - 32 + 0) if False else at("bn", [P, NT, 6], F32, 1568)
    mv = at("mv", [P, NT, 2], F32, 1856)
    lr = at("lr", [P, NT, 2], F32, 2144)
    lt = at("lt", [P, NT, 2], F32, 2432)
    bsT = at("bsT", [P, 8], F32, 3104)
    bfc = at("bfc", [NH2, 2], F32, 3136)
    onecol = at("onecol", [P, 1], F32, 3168)
    negc = at("negc", [P, NH2, SEQ], F32, O_X)
    o2 = at("o2", [P, NT, HALF], F32, O_X + 32768)
    ex2 = at("ex2", [P, 3, 1, SEQ], F32, O_X + 49152)
    at2 = at("at2", [P, 3, 4, P], F32, O_H + 65536)
    att2 = Attention("att2", q2, k2, v2, o2, NH2, ST, 0, 1, ex2, at2, bias=negc)
    mah = at("mah", [P, 4, SEQ], F32R, O_X)
    mal = at("mal", [P, 4, SEQ], F32R, O_X + 16384)
    mbh = at("mbh", [P, 4, SEQ], F32R, O_H + 32768)
    mbl = at("mbl", [P, 4, SEQ], F32R, O_H + 49152)
    o = O_H + 65536
    gb_m = at("gb_m", [P, D], F32, o); o += 4096
    junk_m = at("junk_m", [P, HALF], F32, o); o += 2048
    xs_m = at("xs_m", [P, 2, D], F32, O_H)
    gains_a, gains_b = io["out_norm_a_gain_2"][0], io["out_norm_b_gain_2"][0]
    turn_a = Turn("turn_m", NT, lambda i: au[:, i, :], 1, HALF, gb_m[:, 0:HALF], xs_m,
                  lambda b, lo: (mal if lo else mah)[:, b:b + 4, :], lambda i: i * P)
    turn_b = Turn("turn_m", NT, lambda i: o2[:, i, :], 1, HALF, gb_m[:, HALF:D], xs_m,
                  lambda b, lo: (mbl if lo else mbh)[:, b:b + 4, :], lambda i: i * P, turn=1)

    base = [len(plan1)]
    GLU0 = base[0]
    OUT1_0 = GLU0 + 4
    OUT1_N = 2 * NT
    PLAN2_0 = OUT1_0 + OUT1_N
    plan2 = [("a", U_AV, i) for i in range(NT)] + [("a", U_AU, i) for i in range(NT)] \
        + [("q2", U_Q2, m) for m in range(4)] + [("k2", U_K2, m) for m in range(4)] \
        + [("a", U_V2, i) for i in range(NT)]
    OUT2_0 = PLAN2_0 + len(plan2)

    def pe_out(pe, base, units, xa, xb, apart):
        for h in range(2):
            for i in range(NT):
                n = base + h * NT + i
                first, last = i == 0, i == NT - 1

                def work(bank):
                    for k in range(KT_D):
                        t = units[h] + k
                        if first:
                            pe.wait_ge(w_split, t + 1)
                        s = t % NSLOT
                        x, j = (xa, k) if k < 4 else (xb, k - 4)
                        c = slice(i * P, (i + 1) * P)
                        start, stop = (j == 0, j == 3) if apart else (k == 0, k == KT_D - 1)
                        mm = three(pe, ps[:, bank + (k // 4 if apart else 0), :], (x[0][:, j, c], x[1][:, j, c]),
                                   (wh[:, s, :], wl[:, s, :]), start, stop)
                        if last and k < KT_D - 1:
                            mm.then_inc(w_free, 1)
                    if last:
                        pe.drain().then_inc(w_free, 1)
                    return mm
                pe_step(pe, n, work)

    half = sem("mix_half")

    def dve_out_sum(v, base, scale):
        for h in range(2):
            for i in range(NT):
                n = base + h * NT + i
                bank = 3 * (n % 2)
                dst = hbuf[:, i, h * HALF:(h + 1) * HALF]
                v.wait_ge(half, h * NT + i + 1)
                v.scalar_tensor_tensor(dst, ps[:, bank + 1, :], scale(i), dst, ALU.mult, ALU.add)\
                    .then_inc(emptied[n % 2], 1)

    def act_out_half(act, base):
        for h in range(2):
            for i in range(NT):
                n = base + h * NT + i
                act.wait_ge(step_done, n + 1)
                nc.scalar.copy(hbuf[:, i, h * HALF:(h + 1) * HALF], ps[:, 3 * (n % 2), :]).then_inc(half, 1)


    K = {n: i + 1 for i, n in enumerate((
        "turn1", "in1", "rope", "ssmp", "ssm", "att1", "turn_o", "glu", "split_y", "out1", "post0", "turn_h0",
        "mlp1", "post1", "turn_h1", "fgate", "gmlp", "qkv2", "att2", "turn_a", "turn_b", "out2", "post2",
        "turn_h2", "mlp2", "post3"))}
    last = max([v for v in K.values() if v <= stop])

    def until(name):
        return K[name] <= stop

    def col(ap):
        return ap.rearrange("(m p) -> p m", p=P)

    lamt = at("lamt", [P, 4, ST], F32, 3328)
    keepm = at("keepm", [P, P], F32, O_H + 61440)
    xf = at("xf", [P, P], F32, O_FREE + 16640)
    gel, gyhi, gylo, ydone, yst = (sem(n) for n in (
        "gelu_done", "gated_hi", "gated_lo", "y_gated", "y_stats"))
    y3, y3h = sem("y_gained"), sem("y_hi")
    f_w, f_mm, ws_tr, f_x, f_e = (sem(n) for n in (
        "forget_w_split", "forget_logits", "spatial_turned", "forget_abs", "forget_ln"))
    f_c, cst = sem("forget_cumulated"), sem("forget_stored")
    gl_done, ln_done, sp_mm, sp_used = (sem(n) for n in ("gelus", "ln_done", "spatial_mixed", "spatial_used"))
    dve_misc = sem("consts_cast")

    def empty_plan2(eng, cp, parity):
        for j, (kind, u0, m) in enumerate(plan2):
            n = PLAN2_0 + j
            if j < 2 * NT or n % 2 != parity:
                continue
            eng.wait_ge(step_done, n + 1)
            b = 3 * (n % 2)
            if kind == "a":
                ins = cp(v2[:, m, :], ps[:, b, :], 1.0)
            else:
                dst, scale = (q2, ST ** -0.5) if kind == "q2" else (k2, 1.0)
                ins = cp(dst[:, m, :], ps[:, b:b + 2, :].rearrange("p b c -> p (b c)"), scale)
            ins.then_inc(emptied[parity], 1)

    def empty_out2(eng, cp, parity):
        for h in range(2):
            for i in range(NT):
                n = OUT2_0 + h * NT + i
                if n % 2 != parity:
                    continue
                eng.wait_ge(step_done, n + 1)
                cp(hbuf[:, i, h * HALF:(h + 1) * HALF], ps[:, 3 * (n % 2), :], 1.0).then_inc(emptied[parity], 1)

    block = ctx.enter_context(nc.Block())

    @block.sync
    def _(sp):
        load(sp, "x0", x_tok[0:META, 0, :], io["meta"])
        for i in range(NT):
            load(sp, "x", x_tok[:, i + 1, :], rows(io["x"][0], i))
        if not until("in1"):
            return
        sp_weights(sp, 0, min(U_GLU + NSLOT + NRAW, N_BLOCK1) if until("out1") else U_GLU)
        if until("ssm"):
            sp.wait_ge(met, 3 * K["ssmp"])
            sp_ssm(sp)
        if until("out1"):
            sp_weights(sp, min(U_GLU + NSLOT + NRAW, N_BLOCK1), N_BLOCK1)
        if until("post0"):
            sp.wait_ge(met, 3 * K["out1"])
            post[0].sp(sp)
        if until("mlp1"):
            sp.wait_ge(met, 3 * K["turn_h0"])
            mlp1.sp(sp)
        if until("post1"):
            sp_weights(sp, N_BLOCK1, N_BLOCK1 + NRAW)
            sp.wait_ge(met, 3 * K["mlp1"])
            post[1].sp(sp)
        if until("gmlp"):
            sp_weights(sp, N_BLOCK1 + NRAW, len(stream))
        if until("post2"):
            sp.wait_ge(met, 3 * K["out2"])
            post[2].sp(sp)
        if until("mlp2"):
            sp.wait_ge(met, 3 * K["turn_h2"])
            mlp2.sp(sp)
        if until("post3"):
            sp.wait_ge(met, 3 * K["mlp2"])
            post[3].sp(sp)
            sp.wait_ge(sem("stored"), stored[0])

    @block.gpsimd
    def _(pool):
        if until("in1"):
            pool_weights(pool, 0, N_BLOCK1 if until("out1") else U_GLU)
        if until("mlp1"):
            pool.wait_ge(met, 3 * K["turn_h0"])
            mlp1.pool(pool)
        if until("gmlp"):
            pool.wait_ge(met, 3 * K["mlp1"])
            pool_weights(pool, N_BLOCK1, len(stream))
        if until("mlp2"):
            pool.wait_ge(met, 3 * K["turn_h2"])
            mlp2.pool(pool)

    @block.tensor
    def _(pe):
        k = [0]

        def done():
            k[0] += 1
            meet(pe, k[0])
            return k[0] >= last

        loaded(pe, "ident")
        turn1.pe(pe)
        if done():
            return
        pe_plan(pe, plan1, BASE1, (x1h, x1l), x1k)
        if done():
            return
        loaded(pe, "rot")
        pe_rope(pe)
        if done():
            return
        pe_ssm_params(pe)
        if done():
            return
        pe_ssm(pe)
        if done():
            return
        att1.pe(pe)
        if done():
            return
        turn_o.pe(pe)
        if done():
            return
        pe.wait_ge(gylo, 4)
        for m in range(4):
            pe_step(pe, GLU0 + m, fm_work(pe, U_GLU, 4, m, (gyh, gyl), 0, SEQ))
        if done():
            return
        for i in range(NT):
            for c in range(4):
                mm = pe.matmul(ps[:, 6, i:i + 1], ysq[:, c, i * P:(i + 1) * P], ones[:, 0:1],
                               start=c == 0, stop=c == 3, skip_group_check=True)
        mm.then_inc(yst, 1)
        if done():
            return
        pe_out(pe, OUT1_0, U_O1, (oth, otl), (gyh, gyl), True)
        if done():
            return
        if done():
            return
        turn_h[0].pe(pe)
        if done():
            return
        mlp1.pe(pe)
        if done():
            return
        if done():
            return
        turn_h[1].pe(pe)
        if done():
            return
        pe.wait_ge(f_w, 1)
        for h in range(2):
            for c in range(KT_D):
                cc = slice(h * HALF, (h + 1) * HALF)
                mm = three(pe, ps[:, h, :], (wfh[:, c, :], wfl[:, c, :]), (xh[:, c, cc], xl[:, c, cc]),
                           c == 0, c == KT_D - 1)
        mm.then_inc(f_mm, 1)
        loaded(pe, "wsp", 8)
        for g in range(8):
            t = pe.transpose(ps[:, 2 + g // 4, (g % 4) * P:(g % 4 + 1) * P], wsp[:, g, :], ident[:, :])
        t.then_inc(ws_tr, 1)
        if done():
            return
        xk = [(xh[:, c, :], xl[:, c, :]) for c in range(KT_D)]
        pe_plan(pe, plan2[0:2 * NT], PLAN2_0, (xh, xl), xk)
        for i in range(NT):
            pe.wait_ge(ln_done, i + 1)
            if i >= 2:
                pe.wait_ge(sp_used, i - 1)
            for g in range(8):
                mm = pe.matmul(ps[:, 6 + i % 2, g * ST:(g + 1) * ST], wsT[:, g, :], av[:, i, g * ST:(g + 1) * ST],
                               start=True, stop=True)
            mm.then_inc(sp_mm, 1)
        if done():
            return
        pe_plan(pe, plan2[2 * NT:], PLAN2_0 + 2 * NT, (xh, xl), xk)
        if done():
            return
        att2.pe(pe)
        if done():
            return
        turn_a.pe(pe)
        if done():
            return
        turn_b.pe(pe)
        if done():
            return
        pe_out(pe, OUT2_0, U_O2, (mah, mal), (mbh, mbl), False)
        if done():
            return
        if done():
            return
        turn_h[2].pe(pe)
        if done():
            return
        mlp2.pe(pe)
        if done():
            return
        done()

    @block.scalar
    def _(act):
        k = [0]

        def done():
            k[0] += 1
            meet(act, k[0])
            return k[0] >= last

        load(act, "ident", ident[:, :], io["c_ident"])
        load(act, "gb1", gb1[:, :], rowb(io["pre_mix_g"][0]))
        load(act, "rot", rotT[:, :], io["c_rot"])
        load(act, "maskf", xf[:, :], io["c_mask"])

        def wait_x(eng, i):
            if i == 0:
                loaded(eng, "x0")
            if i == 1:
                loaded(eng, "x", NT)
        act.wait_ge(dve_misc, 1)
        turn1.act(act, junk1, wait_x)
        if done():
            return
        load(act, "rope", rope_c[:, :], io["c_cos"])
        load(act, "rope", rope_s[:, :], io["c_sin"])
        empty_plan1(act, act_cp, 1)
        if done():
            return
        if done():
            return
        sp_ssm_params(act)
        act_ssm_params(act)
        if done():
            return
        load_us(act)
        act_ssm(act)
        if done():
            return
        for j in range(2):
            act.wait_ge(b_yo[j], 16 * TC * NB // 2)
        load(act, "yg", yg[:, :, :, :].rearrange("p m t c -> p m (t c)"),
             yd.rearrange("(m p) t c -> p m (t c)", p=P))
        for j, name in enumerate(("lambda_q1", "lambda_k1", "lambda_q2", "lambda_k2")):
            load(act, "lam", lamt[:, j, :], rowb(io[name][0]))
        with nc.allow_non_contiguous_dma("short columns"):
            load(act, "cols", bcol[:, 0:4], col(io["b_glu"][0]))
            load(act, "cols", sgcol[:, :], col(io["ssm_out_g"][0]))
        att1.act(act)
        if done():
            return
        for h in range(NH1):
            load(act, "gb_o", gb_o[:, h * P:(h + 1) * P], rowb(io["subln_g"][0]))
        turn_o.act(act, junk_o)
        if done():
            return
        loaded(act, "yg")
        loaded(act, "cols", 2)
        for m in range(4):
            nc.scalar.activation(gy[:, m, :].rearrange("p (c t) -> p t c", t=TC), yg[:, m, :, MCH:NCH],
                                 ACT.Gelu).then_inc(gel, 1)
            act.wait_ge(gel, m + 1)
            nc.scalar.copy(gyh[:, m, :], gy[:, m, :]).then_inc(gyhi, 1)
        for m in range(4):
            n = GLU0 + m
            act.wait_ge(step_done, n + 1)
            if m >= 2:
                act.wait_ge(ydone, m - 1)
            b = 3 * (n % 2)
            nc.scalar.activation(sig[:, m % 2, :], ps[:, b:b + 2, :].rearrange("p b c -> p (b c)"), ACT.Sigmoid,
                                 bias=bcol[:, m:m + 1]).then_inc(emptied[n % 2], 1)
        if done():
            return
        for m in range(4):
            act.wait_ge(y3, m + 1)
            nc.scalar.copy(gyh[:, m, :], gy[:, m, :]).then_inc(y3h, 1)
        if done():
            return
        act_out_half(act, OUT1_0)
        if done():
            return

        def do_post(n):
            load(act, "gb_b", gb_b[:, :], rowb(post_gain[n]))
            post[n].act(act, junk_b)

        def do_turn(n):
            load(act, "gb_c", gb_c[:, :], rowb(turn_gain[n]))
            turn_h[n].act(act, junk_b)

        do_post(0)
        if done():
            return
        do_turn(0)
        if done():
            return
        mlp1.act(act)
        if done():
            return
        do_post(1)
        if done():
            return
        do_turn(1)
        if done():
            return
        with nc.allow_non_contiguous_dma("short rows"):
            load(act, "wf", wfr[:, :, :], w_in2[:, 2560:2568].rearrange("(k p) c -> p k c", p=P))
            load(act, "bf", bfc[:, 0:1], io["b_forget_2"].rearrange("a h -> h a"))
            load(act, "bs", bsT[:, :], io["b_spatial_2"][0].rearrange("g t -> t g"))
        load(act, "lng", lng[:, :], rowb(io["ln_v_gain_2"][0]))
        load(act, "lng", lnb[:, :], rowb(io["ln_v_bias_2"][0]))
        load(act, "keep", keepm[:, :], io["c_keep"])
        for g in range(8):
            load(act, "wsp", wsp[:, g, :], io["w_spatial_2"][0, g])
        act.wait_ge(f_x, 1)
        nc.scalar.activation(fl_b[:, :], fl_b[:, :], ACT.Exp).then_inc(f_e, 1)
        act.wait_ge(f_e, 1)
        nc.scalar.activation(fl_b[:, :], fl_b[:, :], ACT.Ln, bias=1.0).then_inc(f_e, 1)
        act.wait_ge(f_c, 1)
        act.dma_start(cd, fl_a[:, :]).then_inc(cst, 16)
        act.wait_ge(cst, 16)
        if done():
            return
        for j in range(2 * NT):
            n = PLAN2_0 + j
            act.wait_ge(step_done, n + 1)
            dst = av if j < NT else au
            nc.scalar.activation(dst[:, j % NT, :], ps[:, 3 * (n % 2), :], ACT.Gelu).then_inc(emptied[n % 2], 1)
            if j == NT - 1:
                act.drain().then_inc(gl_done, 1)
        act.drain().then_inc(gl_done, 1)
        if done():
            return
        empty_plan2(act, act_cp, 1)
        if done():
            return
        for h in range(NH2):
            load(act, "negc", negc[:, h, :], rowb(cd[h]))
        att2.act(act)
        if done():
            return
        load(act, "gb_m", gb_m[:, 0:HALF], rowb(gains_a))
        load(act, "gb_m", gb_m[:, HALF:D], rowb(gains_b))
        turn_a.act(act, junk_m)
        if done():
            return
        turn_b.act(act, junk_m)
        if done():
            return
        empty_out2(act, act_cp, 1)
        if done():
            return
        do_post(2)
        if done():
            return
        do_turn(2)
        if done():
            return
        mlp2.act(act)
        if done():
            return
        do_post(3)
        done()

    @block.vector
    def _(v):
        k = [0]
        link = chain(v, "vector_chain")

        def done():
            k[0] += 1
            meet(v, k[0])
            return k[0] >= last

        link(v.memset(ones[:, :], 1.0))
        link(v.memset(onecol[:, :], 1.0))
        loaded(v, "ident")
        v.tensor_copy(identb[:, :], ident[:, :])
        loaded(v, "maskf")
        v.tensor_copy(maskb[:, :], xf[:, :])
        link(v.memset(stat[:, :, :], 1.0))
        v.drain().then_inc(dve_misc, 1)
        loaded(v, "gb1")
        loaded(v, "x0")
        loaded(v, "x", NT)
        turn1.dve(v, link)
        if done():
            return
        empty_plan1(v, dve_cp, 0)
        if done():
            return
        loaded(v, "rope", 2)
        dve_rope(v, link)
        if done():
            return
        dve_ssm_params(v, link)
        if done():
            return
        dve_ssm(v, link)
        if done():
            return
        loaded(v, "lam", 4)
        for j in range(2):
            link(v.tensor_tensor_reduce(lamt[:, 2 * j, :], lamt[:, 2 * j, :], lamt[:, 2 * j + 1, :], 1.0, 0.0,
                                        ALU.mult, ALU.add, lamv[:, j:j + 1]))
        exact_exp(v, link, lamv[:, 2:4], lamv[:, 0:2], lamt[:, 0, 0:2], lamt[:, 1, 0:2])
        link(v.tensor_tensor(lamv[:, 4:5], lamv[:, 3:4], lamv[:, 2:3], ALU.subtract))
        link(v.tensor_scalar(lamv[:, 4:5], lamv[:, 4:5], -LAM_INIT, None, ALU.add))
        att1.dve(v, link)
        if done():
            return
        loaded(v, "gb_o", NH1)
        turn_o.dve(v, link)
        if done():
            return
        for m in range(4):
            v.wait_ge(gyhi, m + 1)
            v.tensor_tensor(gyl[:, m, :], gy[:, m, :], gyh[:, m, :].bitcast(F32), ALU.subtract).then_inc(gylo, 1)
        for m in range(4):
            n = GLU0 + m
            v.wait_ge(emptied[n % 2], n // 2 + 1)
            v.tensor_tensor(gy[:, m, :], gy[:, m, :], sig[:, m % 2, :], ALU.mult).then_inc(ydone, 1)
            v.wait_ge(ydone, m + 1)
            v.tensor_tensor(ysq[:, m, :], gy[:, m, :], gy[:, m, :], ALU.mult)
        if done():
            return
        for m in range(4):
            v.tensor_scalar(gy[:, m, :], gy[:, m, :], sgcol[:, m:m + 1], None, ALU.mult).then_inc(y3, 1)
        for m in range(4):
            v.wait_ge(y3h, m + 1)
            v.tensor_tensor(gyl[:, m, :], gy[:, m, :], gyh[:, m, :].bitcast(F32), ALU.subtract)
        v.wait_ge(yst, 1)
        link(v.tensor_copy(stat[:, 0:NT, 0], ps[:, 6, 0:NT]))
        rsqrt(v, link, stat[:, 0:NT, 0:1], rst[:, 0:NT, 0:1], tmpa[:, 0:NT, 0:1], tmpb[:, 0:NT, 0:1],
              1.0 / HALF, EPS)
        if done():
            return
        dve_out_sum(v, OUT1_0, lambda i: rst[:, i, 0:1])
        if done():
            return

        def do_post(n):
            loaded(v, "gb_b", n + 1)
            post[n].dve(v, link)

        def do_turn(n):
            loaded(v, "gb_c", n + 1)
            turn_h[n].dve(v, link)

        do_post(0)
        if done():
            return
        do_turn(0)
        if done():
            return
        mlp1.dve(v, link)
        if done():
            return
        do_post(1)
        if done():
            return
        do_turn(1)
        if done():
            return
        loaded(v, "wf")
        link(v.memset(wfp[:, :, :], 0.0))
        link(v.tensor_copy(wfp[:, :, 0:NH2], wfr[:, :, :]))
        link(v.tensor_copy(wfh[:, :, :], wfp[:, :, :]))
        v.tensor_tensor(wfl[:, :, :], wfp[:, :, :], wfh[:, :, :].bitcast(F32), ALU.subtract).then_inc(f_w, 1)
        v.wait_ge(f_mm, 1)
        loaded(v, "bf")
        link(v.tensor_scalar(fl_a[:, :], ps[0:NH2, 0:2, :].rearrange("p b c -> p (b c)"), bfc[:, 0:1], None, ALU.add))
        v.scalar_tensor_tensor(fl_b[:, :], fl_a[:, :], -1.0, fl_a[:, :], ALU.mult, ALU.min).then_inc(f_x, 1)
        v.wait_ge(ws_tr, 1)
        loaded(v, "keep")
        link(v.tensor_tensor(wsT[:, :, :], ps[:, 2:4, :].rearrange("p b (g t) -> p (b g) t", t=P),
                             bc(keepm[:, :], 1, 8), ALU.mult))
        v.wait_ge(f_e, 2)
        link(v.scalar_tensor_tensor(fl_a[:, :], fl_a[:, :], 0.0, fl_b[:, :], ALU.min, ALU.subtract))
        link(v.tensor_tensor_scan(fl_c[:, :], onecol[0:NH2, 0:1].broadcast_to([NH2, SEQ]), fl_a[:, :], 0.0,
                                  ALU.mult, ALU.add))
        v.tensor_scalar(fl_a[:, :], fl_c[:, :], -1.0, None, ALU.mult).then_inc(f_c, 1)
        if done():
            return
        v.wait_ge(gl_done, 1)
        loaded(v, "lng", 2)
        loaded(v, "bs")
        for i in range(NT):
            link(v.bn_stats(bn[:, i, :], av[:, i, :]))
            link(v.bn_aggr(mv[:, i, :], bn[:, i, :]))
        rsqrt(v, link, mv[:, :, 1:2], lr[:, :, 0:1], lt[:, :, 0:1], lt[:, :, 1:2], 1.0, LN_EPS)
        for i in range(NT):
            link(v.tensor_scalar(av[:, i, :], av[:, i, :], mv[:, i, 0:1], lr[:, i, 0:1], ALU.subtract, ALU.mult))
            link(v.tensor_tensor(av[:, i, :], av[:, i, :], lng[:, :], ALU.mult))
            v.tensor_tensor(av[:, i, :], av[:, i, :], lnb[:, :], ALU.add).then_inc(ln_done, 1)
        v.wait_ge(gl_done, 2)
        for i in range(NT):
            v.wait_ge(sp_mm, i + 1)
            mixed = ps[:, 6 + i % 2, :].rearrange("p (g d) -> p g d", d=ST)
            link(v.tensor_tensor(av[:, i, :].rearrange("p (g d) -> p g d", d=ST), mixed, bc(bsT[:, :], 2, ST),
                                 ALU.add))
            v.tensor_tensor(au[:, i, :], au[:, i, :], av[:, i, :], ALU.mult).then_inc(sp_used, 1)
        if done():
            return
        empty_plan2(v, dve_cp, 0)
        if done():
            return
        loaded(v, "negc", NH2)
        att2.dve(v, link)
        if done():
            return
        loaded(v, "gb_m", 2)
        turn_a.dve(v, link)
        if done():
            return
        turn_b.dve(v, link)
        if done():
            return
        empty_out2(v, dve_cp, 0)
        if done():
            return
        do_post(2)
        if done():
            return
        do_turn(2)
        if done():
            return
        mlp2.dve(v, link)
        if done():
            return
        do_post(3)
        done()


ROT_DIM = ST // 4
ROPE_THETA = 500000.0


def constants():
    import numpy as np

    f = np.float32
    r, c = np.indices((P, P))
    rot = np.zeros((P, P), f)
    half = ROT_DIM // 2
    for b in (0, ST):
        for j in range(half):
            rot[b + j + half, b + j] = -1
            rot[b + j, b + j + half] = 1
    inv = (np.float64(ROPE_THETA) ** (-np.arange(0, ROT_DIM, 2) / ROT_DIM)).astype(f)
    ang = (np.arange(L1, dtype=f)[None, :] * inv[:, None]).astype(np.float64)
    cos, sin = np.ones((P, L1), f), np.zeros((P, L1), f)
    for b in (0, ST):
        for j in range(ROT_DIM):
            cos[b + j] = np.cos(ang[j % half])
            sin[b + j] = np.sin(ang[j % half])
    return {"c_ident": np.eye(P, dtype=f), "c_mask": np.where(c > r, f(NEG), f(0)).astype(f),
            "c_keep": (c >= r).astype(f), "c_rot": rot, "c_cos": cos, "c_sin": sin}


NAMES = """x meta pre_mix_g w_in lambda_q1 lambda_k1 lambda_q2 lambda_k2 subln_g a_re a_im log_dt b_re b_im c_re
c_im d_skip w_glu b_glu ssm_out_g w_out post_mix_g pre_ffn_g w_gate w_up w_down post_ffn_g pre_mix_gain_2 w_in_2
ln_v_gain_2 ln_v_bias_2 w_spatial_2 b_spatial_2 b_forget_2 out_norm_a_gain_2 out_norm_b_gain_2 w_out_2
post_mix_gain_2 pre_ffn_gain_2 w_ffn_in_2 w_ffn_out_2 post_ffn_gain_2""".split()


def kernel(**inputs):
    import numpy as np
    import concourse.bacc as bacc
    from concourse.bass_utils import run_bass_kernel_spmd

    nc = bacc.Bacc("TRN2", target_bir_lowering=False, num_devices=1)
    arrays = {name: np.ascontiguousarray(inputs[name]) for name in NAMES}
    arrays.update(constants())
    io = {n: nc.dram_tensor(f"in_{n}", a.shape, mybir.dt.from_np(a.dtype), kind="ExternalInput").ap()
          for n, a in arrays.items()}
    io["out"] = nc.dram_tensor("out_0", (1, SEQ, D), F32, kind="ExternalOutput").ap()
    build(nc, io)
    r = run_bass_kernel_spmd(nc, [{f"in_{n}": a for n, a in arrays.items()}], core_ids=[0])
    return r.results[0]["out_0"]
```
